# Optimizing a Trainium2 kernel written in Bass

```python
import jax, jax.numpy as jnp
from jax import lax
import numpy as np

D_MODEL = 1024
BATCH = 1
SEQ = 1024
DEPTH = 1

N_MEM = 256
GDN_HEADS = 4
GDN_HEAD_DIM = 128
GDN_CONV = 4
GDN_CHUNK = 64
SWA_HEADS = 8
SWA_HEAD_DIM = 64
DILATED_BRANCHES = ((128, 1), (512, 4), (2048, 16))
SWA_BLOCK = 128
MEM_HEADS = 4
MEM_HEAD_DIM = D_MODEL // MEM_HEADS
D_FF = 2816
EPS = 1e-6

GDN_W = GDN_HEADS * GDN_HEAD_DIM
SWA_W = SWA_HEADS * SWA_HEAD_DIM
MIX_W = GDN_W + SWA_W
IN_SIZES = (GDN_W, GDN_W, GDN_W, GDN_W, GDN_HEADS, GDN_HEADS, SWA_W, SWA_W, SWA_W)
IN_COLS = sum(IN_SIZES)
IN_SPLITS = tuple(int(c) for c in np.cumsum(IN_SIZES)[:-1])

kernel_name = "hybrid_gdn_dilated_alibi_macaron_sandwich"

def rms_norm(x, g):
    xf = x.astype(jnp.float32)
    y = xf * lax.rsqrt(jnp.mean(xf * xf, axis=-1, keepdims=True) + EPS)
    return (y * g.astype(jnp.float32)).astype(x.dtype)

def swiglu(x, w_gate, w_up, w_down):
    return (jax.nn.silu(x @ w_gate) * (x @ w_up)) @ w_down

def l2_normalize(x):
    return x * lax.rsqrt(jnp.sum(x * x, axis=-1, keepdims=True) + EPS)

def causal_depthwise_conv(x, w):
    c = x.shape[-1]
    return lax.conv_general_dilated(
        x, w[:, None, :].astype(x.dtype), window_strides=(1,),
        padding=((GDN_CONV - 1, 0),), dimension_numbers=("NWC", "WIO", "NWC"),
        feature_group_count=c)

def gated_delta_chunked(q, k, v, g, beta):
    b_, h_, s_, dk = q.shape
    dv = v.shape[-1]
    c = GDN_CHUNK
    n = s_ // c
    q = q.reshape(b_, h_, n, c, dk)
    k = k.reshape(b_, h_, n, c, dk)
    v = v.reshape(b_, h_, n, c, dv)
    g = jnp.cumsum(g.reshape(b_, h_, n, c), axis=-1)
    beta = beta.reshape(b_, h_, n, c)
    idx = jnp.arange(c)
    tril = idx[:, None] >= idx[None, :]
    strict = idx[:, None] > idx[None, :]
    decay = jnp.exp(jnp.where(tril, g[..., :, None] - g[..., None, :], -jnp.inf))
    k_beta = k * beta[..., None]
    v_beta = v * beta[..., None]
    a = jnp.where(strict, jnp.einsum("bhncd,bhnsd->bhncs", k_beta, k) * decay, 0.0)
    eye = jnp.eye(c, dtype=q.dtype)
    t_mat = lax.linalg.triangular_solve(eye + a, jnp.broadcast_to(eye, a.shape),
                                        left_side=True, lower=True, unit_diagonal=True)
    u = t_mat @ v_beta
    w = t_mat @ (k_beta * jnp.exp(g)[..., None])
    qk = jnp.where(tril, jnp.einsum("bhncd,bhnsd->bhncs", q, k) * decay, 0.0)
    q_dec = q * jnp.exp(g)[..., None]
    k_dec = k * jnp.exp(g[..., -1:] - g)[..., None]
    g_last = jnp.exp(g[..., -1])

    def step(state, xs):
        u_c, w_c, qk_c, qd_c, kd_c, gl_c = xs
        v_new = u_c - w_c @ state
        o_c = qd_c @ state + qk_c @ v_new
        state = state * gl_c[..., None, None] + jnp.einsum("bhcd,bhce->bhde", kd_c, v_new)
        return state, o_c

    xs = tuple(jnp.moveaxis(t, 2, 0) for t in (u, w, qk, q_dec, k_dec, g_last))
    state0 = jnp.zeros((b_, h_, dk, dv), q.dtype)
    _, o = lax.scan(step, state0, xs)
    return jnp.moveaxis(o, 0, 2).reshape(b_, h_, s_, dv)

def gdn_mixer(q, k, v, z, a, b, conv_w, a_log, dt_bias, norm_g):
    b_, s_, _ = q.shape
    qkv = jax.nn.silu(causal_depthwise_conv(jnp.concatenate([q, k, v], axis=-1), conv_w))
    q, k, v = jnp.split(qkv.astype(jnp.float32), 3, axis=-1)
    heads = lambda t: t.reshape(b_, s_, GDN_HEADS, GDN_HEAD_DIM).transpose(0, 2, 1, 3)
    q = l2_normalize(heads(q)) * (GDN_HEAD_DIM ** -0.5)
    k = l2_normalize(heads(k))
    v = heads(v)
    beta = jax.nn.sigmoid(b.astype(jnp.float32)).transpose(0, 2, 1)
    g = -jnp.exp(a_log.astype(jnp.float32)) * jax.nn.softplus(
        a.astype(jnp.float32) + dt_bias.astype(jnp.float32))
    g = g.transpose(0, 2, 1)
    o = gated_delta_chunked(q, k, v, g, beta).transpose(0, 2, 1, 3)
    zf = z.astype(jnp.float32).reshape(b_, s_, GDN_HEADS, GDN_HEAD_DIM)
    o = o * lax.rsqrt(jnp.mean(o * o, axis=-1, keepdims=True) + EPS)
    o = o * norm_g.astype(jnp.float32) * jax.nn.silu(zf)
    return o.reshape(b_, s_, GDN_W).astype(q.dtype if False else z.dtype)

def dilated_branch(q, k, v, slopes, window, dilation):
    b_, h_, s_, dh = q.shape
    d = dilation
    n_back = window // dilation
    sub_len = s_ // d
    nb = -(-sub_len // SWA_BLOCK)
    lp = nb * SWA_BLOCK

    def gather_stride(t):
        t = t.reshape(b_, h_, sub_len, d, dh).transpose(0, 1, 3, 2, 4)
        return jnp.pad(t, ((0, 0), (0, 0), (0, 0), (0, lp - sub_len), (0, 0)))

    def kv_band(t):
        tb = t.reshape(b_, h_, d, nb, SWA_BLOCK, dh)
        prev = jnp.pad(tb, ((0, 0), (0, 0), (0, 0), (1, 0), (0, 0), (0, 0)))[:, :, :, :-1]
        return jnp.concatenate([prev, tb], axis=4)

    qb = gather_stride(q).reshape(b_, h_, d, nb, SWA_BLOCK, dh)
    kb = kv_band(gather_stride(k))
    vb = kv_band(gather_stride(v))
    s = jnp.einsum("bhrnqd,bhrnkd->bhrnqk", qb, kb) * (dh ** -0.5)
    p_idx = jnp.arange(SWA_BLOCK)
    c_idx = jnp.arange(2 * SWA_BLOCK)
    blk = jnp.arange(nb)
    delta = p_idx[:, None] + SWA_BLOCK - c_idx[None, :]
    key_pos = blk[:, None] * SWA_BLOCK + c_idx[None, :] - SWA_BLOCK
    valid = (delta >= 0)[None] & (delta <= n_back)[None] & (key_pos[:, None, :] >= 0)
    alibi = -slopes[:, None, None, None, None] * (dilation * delta).astype(jnp.float32)
    s = jnp.where(valid, s + alibi, -jnp.inf)
    m = jnp.max(s, axis=-1, keepdims=True)
    e = jnp.exp(s - m)
    l = jnp.sum(e, axis=-1, keepdims=True)
    o = jnp.einsum("bhrnqk,bhrnkd->bhrnqd", e, vb) / l
    lse = (m + jnp.log(l))[..., 0]
    o = o.reshape(b_, h_, d, lp, dh)[:, :, :, :sub_len].transpose(0, 1, 3, 2, 4).reshape(b_, h_, s_, dh)
    lse = lse.reshape(b_, h_, d, lp)[:, :, :, :sub_len].transpose(0, 1, 3, 2).reshape(b_, h_, s_)
    return o, lse

def dilated_mixer(q, k, v):
    b_, s_, _ = q.shape
    heads = lambda t: t.reshape(b_, s_, SWA_HEADS, SWA_HEAD_DIM).transpose(0, 2, 1, 3).astype(jnp.float32)
    qh, kh, vh = heads(q), heads(k), heads(v)
    slopes = 2.0 ** (-8.0 * jnp.arange(1, SWA_HEADS + 1, dtype=jnp.float32) / SWA_HEADS)
    outs, lses = [], []
    for window, dilation in DILATED_BRANCHES:
        o_i, lse_i = dilated_branch(qh, kh, vh, slopes, window, dilation)
        outs.append(o_i)
        lses.append(lse_i)
    wts = jax.nn.softmax(jnp.stack(lses, axis=0), axis=0)
    o = jnp.einsum("gbhs,gbhsd->bhsd", wts, jnp.stack(outs, axis=0))
    return o.transpose(0, 2, 1, 3).reshape(b_, s_, SWA_W).astype(q.dtype)

def memory_cross_attention(h, mem_n, wq, wk, wv, wo):
    b_, s_, _ = h.shape
    m_ = mem_n.shape[1]
    q = (h @ wq).reshape(b_, s_, MEM_HEADS, MEM_HEAD_DIM)
    k = (mem_n @ wk).reshape(b_, m_, MEM_HEADS, MEM_HEAD_DIM)
    v = (mem_n @ wv).reshape(b_, m_, MEM_HEADS, MEM_HEAD_DIM)
    s = jnp.einsum("bshd,bmhd->bhsm", q, k).astype(jnp.float32) * (MEM_HEAD_DIM ** -0.5)
    p = jax.nn.softmax(s, axis=-1).astype(v.dtype)
    o = jnp.einsum("bhsm,bmhd->bshd", p, v).reshape(b_, s_, D_MODEL)
    return o @ wo

def setup_inputs(seed: int = 0) -> dict:
    key = jax.random.key(seed)
    ks = iter(jax.random.split(key, 40))
    nrm = lambda shape, fan_in: jax.random.normal(next(ks), shape, jnp.float32) * (fan_in ** -0.5)
    gain = lambda n: 1.0 + 0.05 * jax.random.normal(next(ks), (DEPTH, n), jnp.float32)
    x = jax.random.normal(next(ks), (BATCH, SEQ, D_MODEL), jnp.float32)
    mem = jax.random.normal(next(ks), (BATCH, N_MEM, D_MODEL), jnp.float32)
    a_log = jnp.log(jax.random.uniform(next(ks), (DEPTH, GDN_HEADS), jnp.float32, 1.0, 16.0))
    dt = jnp.exp(jax.random.uniform(next(ks), (DEPTH, GDN_HEADS), jnp.float32,
                                    np.log(1e-3), np.log(1e-1)))
    dt_bias = dt + jnp.log(-jnp.expm1(-dt))
    return {
        "x": x,
        "mem": mem,
        "ffn1_pre_g": gain(D_MODEL),
        "ffn1_w_gate": nrm((DEPTH, D_MODEL, D_FF), D_MODEL),
        "ffn1_w_up": nrm((DEPTH, D_MODEL, D_FF), D_MODEL),
        "ffn1_w_down": nrm((DEPTH, D_FF, D_MODEL), D_FF),
        "ffn1_post_g": gain(D_MODEL),
        "mix_pre_g": gain(D_MODEL),
        "w_in": nrm((DEPTH, D_MODEL, IN_COLS), D_MODEL),
        "gdn_conv_w": nrm((DEPTH, GDN_CONV, 3 * GDN_W), GDN_CONV),
        "gdn_a_log": a_log,
        "gdn_dt_bias": dt_bias,
        "gdn_norm_g": gain(GDN_HEAD_DIM),
        "w_out": nrm((DEPTH, MIX_W, D_MODEL), MIX_W),
        "mix_post_g": gain(D_MODEL),
        "mem_pre_g": gain(D_MODEL),
        "mem_kv_g": gain(D_MODEL),
        "mem_wq": nrm((DEPTH, D_MODEL, D_MODEL), D_MODEL),
        "mem_wk": nrm((DEPTH, D_MODEL, D_MODEL), D_MODEL),
        "mem_wv": nrm((DEPTH, D_MODEL, D_MODEL), D_MODEL),
        "mem_wo": nrm((DEPTH, D_MODEL, D_MODEL), D_MODEL),
        "mem_post_g": gain(D_MODEL),
        "ffn2_pre_g": gain(D_MODEL),
        "ffn2_w_gate": nrm((DEPTH, D_MODEL, D_FF), D_MODEL),
        "ffn2_w_up": nrm((DEPTH, D_MODEL, D_FF), D_MODEL),
        "ffn2_w_down": nrm((DEPTH, D_FF, D_MODEL), D_FF),
        "ffn2_post_g": gain(D_MODEL),
    }

def reference(x, mem, ffn1_pre_g, ffn1_w_gate, ffn1_w_up, ffn1_w_down, ffn1_post_g,
              mix_pre_g, w_in, gdn_conv_w, gdn_a_log, gdn_dt_bias, gdn_norm_g, w_out, mix_post_g,
              mem_pre_g, mem_kv_g, mem_wq, mem_wk, mem_wv, mem_wo, mem_post_g,
              ffn2_pre_g, ffn2_w_gate, ffn2_w_up, ffn2_w_down, ffn2_post_g):
    for l in range(DEPTH):
        f = swiglu(rms_norm(x, ffn1_pre_g[l]), ffn1_w_gate[l], ffn1_w_up[l], ffn1_w_down[l])
        x = x + 0.5 * rms_norm(f, ffn1_post_g[l])
        h = rms_norm(x, mix_pre_g[l])
        proj = h @ w_in[l]
        qa, ka, va, za, aa, ba, qb, kb, vb = jnp.split(proj, IN_SPLITS, axis=-1)
        o_a = gdn_mixer(qa, ka, va, za, aa, ba, gdn_conv_w[l], gdn_a_log[l], gdn_dt_bias[l], gdn_norm_g[l])
        o_b = dilated_mixer(qb, kb, vb)
        mix = jnp.concatenate([o_a, o_b], axis=-1) @ w_out[l]
        x = x + rms_norm(mix, mix_post_g[l])
        c = memory_cross_attention(rms_norm(x, mem_pre_g[l]), rms_norm(mem, mem_kv_g[l]),
                                   mem_wq[l], mem_wk[l], mem_wv[l], mem_wo[l])
        x = x + rms_norm(c, mem_post_g[l])
        f = swiglu(rms_norm(x, ffn2_pre_g[l]), ffn2_w_gate[l], ffn2_w_up[l], ffn2_w_down[l])
        x = x + 0.5 * rms_norm(f, ffn2_post_g[l])
    return x


_drawn_inputs = setup_inputs


def setup_inputs(seed=0):
    import zlib

    import numpy as np

    out = dict(_drawn_inputs(seed))
    spreads = {}
    factors = {'ffn2_pre_g': 2.937, 'ffn2_post_g': 4.208}
    for name, (base, spread) in spreads.items():
        noise = np.random.default_rng([zlib.crc32(name.encode()), seed]).standard_normal(out[name].shape)
        drawn = base * np.exp(spread * noise) if base else spread * noise
        out[name] = __import__('jax').numpy.asarray(drawn.astype(out[name].dtype))
    for name, factor in factors.items():
        out[name] = (out[name] * factor).astype(out[name].dtype)
    return out
```

```python
from contextlib import ExitStack
import math

import concourse.bass as bass
from concourse import mybir

F32 = mybir.dt.float32
F32R = mybir.dt.float32r
I32 = mybir.dt.int32
ACT = mybir.ActivationFunctionType
ALU = mybir.AluOpType
AXX = mybir.AxisListType.X

P = 128
D = 1024
S = 1024
NMEM = 256
DFF = 2816
KT = D // P
TOK = 512
HALVES = S // TOK
TT = TOK // P
FT = DFF // P
CHUNKS = (8, 7, 7)
assert sum(CHUNKS) == FT
EPS = 1e-6

GH, GD = 4, 128
AH, AD = 8, 64
GW = GH * GD
AB0 = 4 * GW
QB0 = AB0 + 2 * GH
LEVELS = (2, 4, 8, 16, 32, 64)
MH, MD = 4, 256
NEG = -1.0e30

FFN_STEPS = sum(CHUNKS) + len(CHUNKS) * (KT // 2)
GDN_STEPS = 2 * GW * 4 // (2 * P) // 2
ATT_STEPS = 3 * AH * AD // (2 * P)
MIX_STEPS = GDN_STEPS + 1 + ATT_STEPS + KT // 2
KV_STEPS = KT
MEM_STEPS = KT
FFN1_0 = 0
MIX_0 = FFN1_0 + HALVES * FFN_STEPS
KV_0 = MIX_0 + HALVES * MIX_STEPS
MEM_0 = KV_0 + KV_STEPS
FFN2_0 = MEM_0 + HALVES * MEM_STEPS
STEPS = FFN2_0 + HALVES * FFN_STEPS

PRE_TILES = (4, 4, 4, 4, 2, 4, 4, 4, 4)
PRE_BASE = [sum(PRE_TILES[:i]) for i in range(len(PRE_TILES))]

N_SMALL = 12
N_CONST = 8 + 3 * (1 + len(LEVELS))
PT_N = (0, AH * TT)


def hybrid_layer(nc, t):
    ctx = ExitStack()
    with ctx:
        def sb(name, shape, dt=F32, scope=ctx):
            return scope.enter_context(nc.sbuf_tensor(name, shape, dt))

        def sem(name):
            return ctx.enter_context(nc.semaphore(name))

        x = sb("x", [P, S // P, D])
        w_raw = sb("w_raw", [P, 2, 2, KT, P])
        w_hi = sb("w_hi", [P, 2, 2, KT, P], F32R)
        w_lo = sb("w_lo", [P, 2, 2, KT, P], F32R)
        h_hi = sb("h_hi", [P, KT, TOK], F32R)
        h_lo = sb("h_lo", [P, KT, TOK], F32R)
        arena = sb("arena", [P, 16, 512])
        xn = arena[:, 0:8, :].rearrange("p (t c) n -> p t (c n)", t=TT)
        oT = arena[:, 8:16, :]
        ident = sb("ident", [P, P])
        ones = sb("ones", [P, P])
        tri_u = sb("tri_u", [P, P])
        tri_s = sb("tri_s", [P, P])
        m_lvl = sb("m_lvl", [P, 1 + len(LEVELS), P])
        g_row = arena[:, 6:8, :].rearrange("p a n -> p (a n)")
        g_pre = sb("g_pre", [P, 5, KT])
        conv_w = sb("conv_w", [P, 12, 4])
        carry = sb("carry", [P, 12, 3])
        ngain = sb("ngain", [P, 1])
        dt_row = sb("dt_row", [P, GH])
        neg_a = sb("neg_a", [P, GH])
        state = sb("state", [P, GH, GD])
        pre_junk = arena[:, 8:10, :].rearrange("p a n -> p (a n)")
        post_junk = arena[:, 0:2, :].rearrange("p a n -> p (a n)")
        post_tmp = arena[:, 2:4, :].rearrange("p a n -> p (a n)")
        yconv = arena[:, 6:8, :]
        ssq_pre = sb("ssq_pre", [P, 34])
        rs_pre = sb("rs_pre", [P, 34])
        ssq_post = sb("ssq_post", [P, 32])
        rs_post = sb("rs_post", [P, 32])
        half_pow = sb("half_pow", [P, 8])
        sm = sb("sm", [P, 24, 16])

        def scoped(specs):
            with ExitStack() as s:
                return [sb(n, sh, dt, s) for n, sh, dt in specs]

        act_hi, act_lo, sg, prod = scoped([
            ("act_hi", [P, 8, TOK], F32R), ("act_lo", [P, 8, TOK], F32R),
            ("sg", [P, 2, TOK], F32), ("prod", [P, 2, TOK], F32)])
        cT, zT, kb0, vn0 = scoped([
            ("cT", [P, 12, TOK], F32), ("zT", [P, GH, TOK], F32),
            ("kb0", [P, 4, TOK], F32), ("vn0", [P, TT, TOK], F32)])
        qmT, kmT, vm, memx = scoped([
            ("qmT", [P, KT, TOK], F32), ("kmT", [P, KT, NMEM], F32),
            ("vm", [P, 2, D], F32), ("memx", [P, 2, D], F32)])
        kb1, vn1, qbT = cT[:, 0:4, :], cT[:, 4:8, :], cT[:, 8:12, :]
        kb = (kb0, kb1)
        vn = (vn0, vn1)
        onat = zT

        def rawc(par):
            return arena[:, 0:8, :].rearrange("p a n -> p (a n)")[:, par * 2 * (TOK + 3):(par + 1) * 2 * (TOK + 3)].rearrange(
                "p (b n) -> p b n", b=2)

        def ptm(hd):
            return arena[:, 4 + 2 * (hd % 2):6 + 2 * (hd % 2), :]

        accp = [[ctx.enter_context(nc.psum_tensor(f"acc{a}{b}", [P, 512], F32)) for b in range(2)]
                for a in range(2)]
        side = ctx.enter_context(nc.psum_tensor("side", [P, 4, 512], F32))

        def bank(n):
            if n % 2:
                return [side[:, 0, :], side[:, 1, :]], side[:, 2, :], side[:, 3, :]
            return [accp[0][0][:], accp[0][1][:]], accp[1][0][:], accp[1][1][:]

        const_in = sem("const_in")
        x_in = sem("x_in")
        mem_in = sem("mem_in")
        grow_in = sem("grow_in")
        mask_st = sem("mask_st")
        neg_rdy = sem("neg_rdy")
        w_landed = [sem("w_landed0"), sem("w_landed1")]
        w_hi_ok = sem("w_hi_ok")
        w_lo_ok = sem("w_lo_ok")
        w_used = sem("w_used")
        act_evac = sem("act_evac")
        acc_free = sem("acc_free")
        act_hi_ok = sem("act_hi_ok")
        act_lo_ok = sem("act_lo_ok")
        dve_seq = sem("dve_seq")
        pre_ssq = sem("pre_ssq")
        pre_v = sem("pre_v")
        pre_rs = sem("pre_rs")
        pre_xn = sem("pre_xn")
        pre_tr = sem("pre_tr")
        pre_hi = sem("pre_hi")
        pre_lo = sem("pre_lo")
        post_tr = sem("post_tr")
        post_ssq = sem("post_ssq")
        post_v = sem("post_v")
        post_rs = sem("post_rs")
        post_x = sem("post_x")
        conv_ok = sem("conv_ok")
        conv_silu = sem("conv_silu")
        S_ = {n: sem(n) for n in (
            "ab_tr ab_sb ab_exp g_ok g_mm g_sb g_e g_be "
            "nat sq ssr v2 rs2 kq_n vb_ok em_x e_ok eb_ok kqt_tr kqt_sb kk a_ok t1 qk_ok u_tr u_sb "
            "as_ok lx lxs ly lz lu lt ks s_scl r_ok vnew vnew_sb o_mm st_ok o_ok o_sq o_ssr o_v o_rs on_ok "
            "on_tr mo_ok mx_hi mx_lo").split()}
        B_ = {n: sem("b_" + n) for n in (
            "vt v_ok di lm bias_i qk smax nmx p_ok rinv pt pt_ok pv o_ok tr hi lo").split()}
        M_ = {n: sem("m_" + n) for n in "kvt vm qk mx nmx p_ok pn pt pt_ok pv hi lo".split()}
        out_ok = sem("out_ok")

        def wcols(w, c0, nk=KT, r0=0):
            return w[0][r0:r0 + nk * P, c0].rearrange("(k p) n -> p k n", p=P)

        def bc_h(v):
            return v.unsqueeze(2).to_broadcast([P, GH, P])

        def bc_m(m):
            return m.unsqueeze(1).to_broadcast([P, GH, P])

        def steps(eng, first, n, body):
            pairs = n // 2
            peeled = pairs if pairs < 2 else int(first == 0)
            for k in range(2 * peeled):
                body(first + k, k, (first + k) % 2)
            if peeled < pairs:
                with eng.Fori(peeled, pairs) as i:
                    body(i * 2 + first, i * 2, first % 2)
                    body(i * 2 + (first + 1), i * 2 + 1, (first + 1) % 2)
            if n % 2:
                body(first + n - 1, n - 1, (first + n - 1) % 2)

        SK = (len(CHUNKS) - 1) * (KT // 2)

        def ffn_skip(base_skip, h, c):
            return base_skip + h * SK + max(0, c - 1) * (KT // 2)

        FFN1_SKIP, MID_SKIP = 0, HALVES * SK
        FFN2_SKIP = MID_SKIP
        FSTEP = [sum(CHUNKS[:c]) + c * (KT // 2) for c in range(len(CHUNKS))]

        block = ctx.enter_context(nc.Block())

        @block.sync
        def _(sp):
            def load(p, par, blocks):
                if not isinstance(p, int) or p >= 2:
                    sp.wait_ge(w_lo_ok, p - 1)
                for dst, src in blocks:
                    sp.dma_start(dst, src).then_inc(w_landed[par], 16)

            def pair(par, nk, a, b):
                return [(w_raw[:, par, 0, 0:nk, :], a), (w_raw[:, par, 1, 0:nk, :], b)]

            def cols(j, k, base=0):
                if isinstance(j, int):
                    return slice(base + (2 * j + k) * P, base + (2 * j + k + 1) * P)
                return bass.ds(j * (2 * P) + (base + k * P), P)

            def ffn(p0, wg, wu, wd, before=None):
                f0 = 0
                for c, nf in enumerate(CHUNKS):
                    def up(p, j, par, f0=f0):
                        cs = slice((f0 + j) * P, (f0 + j + 1) * P) if isinstance(j, int) else bass.ds(j * P + f0 * P, P)
                        load(p, par, pair(par, KT, wcols(wg, cs), wcols(wu, cs)))

                    def down(p, j, par, f0=f0, nf=nf):
                        load(p, par, pair(par, nf, wcols(wd, cols(j, 0), nf, f0 * P),
                                          wcols(wd, cols(j, 1), nf, f0 * P)))
                    if p0 == 0 and c == 0:
                        up(0, 0, 0)
                        for k in range(S // P):
                            sp.dma_start(x[:, k, :], t["x"][0][k * P:(k + 1) * P, :]).then_inc(x_in, 16)
                        up(1, 1, 1)
                        steps(sp, 2, nf - 2, lambda p, j, par: up(p, j + 2, par))
                    else:
                        steps(sp, p0 + FSTEP[c], nf, up)
                    steps(sp, p0 + FSTEP[c] + nf, KT // 2, down)
                    f0 += nf

            def plain(p0, n, w, base=0):
                steps(sp, p0, n, lambda p, j, par: load(p, par, pair(
                    par, KT, wcols(w, cols(j, 0, base)), wcols(w, cols(j, 1, base)))))

            def gain_row(name, p):
                sp.wait_ge(w_used, p + 1)
                sp.dma_start(g_row, t[name][0].partition_broadcast(P)).then_inc(grow_in, 16)

            for h in range(HALVES):
                ffn(FFN1_0 + h * FFN_STEPS, t["ffn1_w_gate"], t["ffn1_w_up"], t["ffn1_w_down"])
                gain_row("ffn1_post_g", FFN1_0 + (h + 1) * FFN_STEPS - 3)
            for h in range(HALVES):
                p0 = MIX_0 + h * MIX_STEPS
                plain(p0, GDN_STEPS, t["w_in"])
                p = p0 + GDN_STEPS
                ab = wcols(t["w_in"], slice(AB0, AB0 + 2 * GH))
                load(p, p % 2, [(w_raw[:, p % 2, 0, 0:4, 0:2 * GH], ab[:, 0:4, :]),
                                (w_raw[:, p % 2, 0, 4:8, 0:2 * GH], ab[:, 4:8, :])])
                plain(p0 + GDN_STEPS + 1, ATT_STEPS, t["w_in"], QB0)
                plain(p0 + GDN_STEPS + 1 + ATT_STEPS, KT // 2, t["w_out"])
                gain_row("mix_post_g", p0 + MIX_STEPS - 3)
            sp.wait_ge(w_used, KV_0)
            sp.wait_ge(B_["lo"], 8)
            sp.dma_start(memx[:], t["mem"][0].rearrange("(t p) d -> p t d", p=P)).then_inc(mem_in, 16)
            plain(KV_0, KT // 2, t["mem_wk"])
            plain(KV_0 + KT // 2, KT // 2, t["mem_wv"])
            for h in range(HALVES):
                plain(MEM_0 + h * MEM_STEPS, KT // 2, t["mem_wq"])
                plain(MEM_0 + h * MEM_STEPS + KT // 2, KT // 2, t["mem_wo"])
                gain_row("mem_post_g", MEM_0 + (h + 1) * MEM_STEPS - 3)
            for h in range(HALVES):
                ffn(FFN2_0 + h * FFN_STEPS, t["ffn2_w_gate"], t["ffn2_w_up"], t["ffn2_w_down"])
                gain_row("ffn2_post_g", FFN2_0 + (h + 1) * FFN_STEPS - 3)
            for tt in range(S // P):
                sp.wait_ge(post_x, 6 * TT + tt + 1)
                sp.dma_start(t["out"][0][tt * P:(tt + 1) * P, :], x[:, tt, :]).then_inc(out_ok, 16)
            sp.wait_ge(out_ok, 16 * S // P)

        @block.gpsimd
        def _(pool):
            n_mask = [0]

            def keep(ins):
                n_mask[0] += 1
                ins.then_inc(mask_st, 1)
                pool.wait_ge(mask_st, n_mask[0])

            pool.dma_start(g_pre[:, 0, :], t["ffn1_pre_g"][0].rearrange("(k p) -> p k", p=P)).then_inc(const_in, 16)
            pool.dma_start(g_pre[:, 1, :], t["mix_pre_g"][0].rearrange("(k p) -> p k", p=P)).then_inc(const_in, 16)
            pool.dma_start(g_pre[:, 2, :], t["mem_pre_g"][0].rearrange("(k p) -> p k", p=P)).then_inc(const_in, 16)
            pool.dma_start(g_pre[:, 3, :], t["ffn2_pre_g"][0].rearrange("(k p) -> p k", p=P)).then_inc(const_in, 16)
            pool.dma_start(g_pre[:, 4, :], t["mem_kv_g"][0].rearrange("(k p) -> p k", p=P)).then_inc(const_in, 16)
            for j in range(4):
                pool.dma_start(conv_w[:, :, j], t["gdn_conv_w"][0][j].rearrange("(k p) -> p k", p=P)).then_inc(const_in, 16)
            pool.dma_start(ngain[:], t["gdn_norm_g"][0].rearrange("(p a) -> p a", a=1)).then_inc(const_in, 16)
            pool.dma_start(dt_row[:], t["gdn_dt_bias"][0].partition_broadcast(P)).then_inc(const_in, 16)
            pool.dma_start(neg_a[:], t["gdn_a_log"][0].partition_broadcast(P)).then_inc(const_in, 16)
            keep(pool.memset(half_pow[:], -0.5))
            keep(pool.memset(ones[:], 1.0))
            keep(pool.memset(carry[:], 0.0))
            keep(pool.memset(state[:], 0.0))
            keep(pool.memset(ident[:], 0.0))
            keep(pool.affine_select(out=ident[:], in_=ident[:], compare_op=ALU.not_equal, fill=1.0,
                                    base=0, pattern=[[-1, P]], channel_multiplier=1))
            keep(pool.affine_select(out=tri_u[:], in_=ones[:], compare_op=ALU.is_ge, fill=0.0,
                                    base=0, pattern=[[1, P]], channel_multiplier=-1))
            keep(pool.affine_select(out=tri_s[:], in_=ones[:], compare_op=ALU.is_gt, fill=0.0,
                                    base=0, pattern=[[-1, P]], channel_multiplier=1))
            for n, s in enumerate((1,) + LEVELS):
                v = m_lvl[:, n, :].rearrange("p (a t) -> p a t", t=2 * s)
                na = P // (2 * s)
                keep(pool.affine_select(out=v, in_=ones[:].rearrange("p (a t) -> p a t", t=2 * s),
                                        compare_op=ALU.is_ge, fill=0.0, base=-s,
                                        pattern=[[-2 * s, na], [0, 2 * s]], channel_multiplier=1))
                keep(pool.affine_select(out=v, in_=v, compare_op=ALU.is_ge, fill=0.0, base=2 * s - 1,
                                        pattern=[[2 * s, na], [0, 2 * s]], channel_multiplier=-1))
                keep(pool.affine_select(out=v, in_=v, compare_op=ALU.is_ge, fill=0.0, base=s - 1,
                                        pattern=[[0, na], [-1, 2 * s]], channel_multiplier=0))
            assert n_mask[0] == N_CONST

            def roots(ssq, rs, n0, n, own, own_n, done, scale=1.0 / D, eps=EPS):
                pool.tensor_scalar(rs[:, n0:n0 + n], ssq[:, n0:n0 + n], scale, eps, ALU.mult, ALU.add).then_inc(own, 1)
                pool.wait_ge(own, own_n)
                pool.tensor_tensor(rs[:, n0:n0 + n], rs[:, n0:n0 + n], half_pow[:, 0:n], ALU.pow).then_inc(done, 1)

            def pre(q):
                pool.wait_ge(pre_ssq, PRE_BASE[q] + PRE_TILES[q])
                roots(ssq_pre, rs_pre, PRE_BASE[q], PRE_TILES[q], pre_v, q + 1, pre_rs)

            def post(r):
                for k in range(TT):
                    n = r * TT + k
                    pool.wait_ge(post_ssq, n + 1)
                    roots(ssq_post, rs_post, n, 1, post_v, n + 1, post_rs)

            def gdn(h):
                for l in range(TT):
                    n = h * TT + l
                    pool.wait_ge(S_["ssr"], 2 * n + 2)
                    pool.tensor_scalar(sm[:, 12, 0:4], sm[:, 10, 0:4], float(GD), EPS * GD, ALU.mult, ALU.add).then_inc(S_["v2"], 1)
                    pool.tensor_scalar(sm[:, 12, 4:8], sm[:, 10, 4:8], 1.0, EPS, ALU.mult, ALU.add).then_inc(S_["v2"], 1)
                    pool.wait_ge(S_["v2"], 2 * n + 2)
                    pool.tensor_tensor(sm[:, 13, 0:8], sm[:, 12, 0:8], half_pow[:, 0:8], ALU.pow).then_inc(S_["rs2"], 1)
                    E, Eb, Eu, kn, kd = (arena[:, i, :].rearrange("p (h c) -> p h c", h=GH) for i in (4, 5, 6, 1, 3))
                    pool.wait_ge(S_["e_ok"], n + 1)
                    pool.tensor_tensor(Eb, E, bc_m(tri_s[:]), ALU.mult).then_inc(S_["eb_ok"], 1)
                    pool.tensor_tensor(Eu, E, bc_m(tri_u[:]), ALU.mult).then_inc(S_["eb_ok"], 1)
                    pool.wait_ge(S_["eb_ok"], 4 * n + 1)
                    pool.tensor_tensor(Eb, Eb, bc_h(sm[:, 1, l * 4:l * 4 + 4]), ALU.mult).then_inc(S_["eb_ok"], 1)
                    pool.wait_ge(S_["kq_n"], 2 * n + 2)
                    pool.tensor_tensor(kd, kn, bc_h(sm[:, 6, l * 4:l * 4 + 4]), ALU.mult).then_inc(S_["eb_ok"], 1)
                    A = arena[:, 5, :].rearrange("p (h c) -> p h c", h=GH)
                    pool.wait_ge(S_["a_ok"], n + 1)
                    for v in range(len(LEVELS)):
                        if v >= 2:
                            pool.wait_ge(S_["lx"], 6 * n + v - 1)
                        pool.tensor_tensor(arena[:, 12 + v % 2, :].rearrange("p (h c) -> p h c", h=GH), A,
                                           bc_m(m_lvl[:, v + 1, :]), ALU.mult).then_inc(S_["as_ok"], 1)
                    pool.wait_ge(S_["ks"], n + 1)
                    pool.tensor_tensor(state[:], state[:], bc_h(sm[:, 5, l * 4:l * 4 + 4]), ALU.mult).then_inc(S_["s_scl"], 1)
                    pool.wait_ge(S_["o_ssr"], n + 1)
                    pool.tensor_scalar(sm[:, 14, 0:4], sm[:, 14, 4:8], 1.0 / GD, EPS, ALU.mult, ALU.add).then_inc(S_["o_v"], 1)
                    pool.wait_ge(S_["o_v"], n + 1)
                    pool.tensor_tensor(sm[:, 14, 8:12], sm[:, 14, 0:4], half_pow[:, 0:4], ALU.pow).then_inc(S_["o_rs"], 1)

            def att(h):
                pool.wait_ge(S_["mo_ok"], (h + 1) * TT)
                pool.iota(arena[:, 0:2, :].rearrange("p a n -> p (a n)").bitcast(I32), pattern=[[-1, S]],
                          base=S - P, channel_multiplier=1).then_inc(B_["di"], 1)
                for hd in range(AH):
                    n = h * AH + hd
                    bias = arena[:, 2 * (hd % 2):2 * (hd % 2) + 2, :].rearrange("p a n -> p (a n)")
                    if hd >= 2:
                        pool.wait_ge(B_["smax"], 4 * (n - 1))
                    else:
                        pool.wait_ge(B_["lm"], h + 1)
                    pool.iota(bias, pattern=[[1, S]], base=P - S, channel_multiplier=-1,
                              allow_small_or_imprecise_dtypes=True).then_inc(B_["bias_i"], 1)
                    pool.wait_ge(B_["bias_i"], 3 * n + 1)
                    pool.tensor_scalar(bias, bias, 8.0 * 2.0 ** -(hd + 1), 0.0, ALU.mult, ALU.add).then_inc(B_["bias_i"], 1)
                    pool.wait_ge(B_["bias_i"], 3 * n + 2)
                    pool.wait_ge(B_["lm"], h + 1)
                    pool.tensor_tensor(bias, bias, arena[:, 12:14, :].rearrange("p a n -> p (a n)"), ALU.add).then_inc(B_["bias_i"], 1)

            for h in range(HALVES):
                pre(h)
                post(h)
            for h in range(HALVES):
                pre(2 + h)
                gdn(h)
                att(h)
                post(2 + h)
            pre(4)
            for h in range(HALVES):
                pre(5 + h)
                post(4 + h)
            for h in range(HALVES):
                pre(7 + h)
                post(6 + h)

        @block.tensor
        def _(pe):
            def mm3(out, k_out, hi, lo, xh, xl, nk):
                for k in range(nk):
                    pe.matmul(out, hi[:, k, :], xh[:, k, :], start=(k == 0), stop=False)
                    pe.matmul(out, hi[:, k, :], xl[:, k, :], start=False, stop=False)
                    last = pe.matmul(out, lo[:, k, :], xh[:, k, :], start=False, stop=(k == nk - 1))
                return last

            def step(p, par, xh, xl, nk, n=TOK, blocks=2):
                pe.wait_ge(w_lo_ok, p + 1)
                if not isinstance(p, int) or p >= 2:
                    pe.wait_ge(acc_free, p - 1)
                for b in range(blocks):
                    last = mm3(accp[par][b][:, 0:n], b, w_hi[:, par, b], w_lo[:, par, b], xh, xl, nk)
                last.then_inc(w_used, 1)

            def pre(q):
                nt = PRE_TILES[q]
                pe.wait_ge(pre_xn, PRE_BASE[q] + nt)
                for k in range(KT):
                    m = q * KT + k
                    if k >= 2:
                        pe.wait_ge(pre_lo, m - 1)
                    for tt in range(nt):
                        last = pe.transpose(side[:, k % 2, tt * P:(tt + 1) * P], xn[:, tt, k * P:(k + 1) * P], ident[:])
                    last.then_inc(pre_tr, 1)
                pe.wait_ge(pre_lo, q * KT + KT)

            def post(r, last_step):
                pe.wait_ge(acc_free, last_step + 1)
                for k in range(TT):
                    n = r * TT + k
                    if k >= 2:
                        pe.wait_ge(post_x, n - 1)
                    for d in range(KT):
                        last = pe.transpose(side[:, 2 * (k % 2) + d // 4, (d % 4) * P:(d % 4 + 1) * P],
                                            oT[:, d, k * P:(k + 1) * P], ident[:])
                    last.then_inc(post_tr, 1)
                pe.wait_ge(post_x, (r + 1) * TT)

            def ffn(p0, u0):
                for c, nf in enumerate(CHUNKS):
                    steps(pe, p0 + FSTEP[c], nf, lambda p, j, par: step(p, par, h_hi, h_lo, KT))
                    u0 += nf
                    pe.wait_ge(act_lo_ok, u0)
                    steps(pe, p0 + FSTEP[c] + nf, KT // 2,
                          lambda p, j, par: step(p, par, act_hi, act_lo, nf))
                return u0

            def heads(buf):
                return buf.rearrange("p (h c) -> p h c", h=GH)

            def gdn(h):
                pe.wait_ge(acc_free, MIX_0 + h * MIX_STEPS + GDN_STEPS + 1)
                for l in range(TT):
                    last = pe.transpose(side[:, 0, l * 8:l * 8 + 8], arena[0:8, 15, l * P:(l + 1) * P], ident[0:8, 0:8])
                last.then_inc(S_["ab_tr"], 1)
                pe.wait_ge(S_["g_ok"], h + 1)
                pe.matmul(side[:, 1, 0:16], tri_u[:], sm[:, 0, :], start=True, stop=True)
                pe.matmul(side[:, 2, 0:16], ones[:], sm[:, 0, :], start=True, stop=True).then_inc(S_["g_mm"], 1)
                pe.wait_ge(S_["g_be"], h + 1)
                for l in range(TT):
                    n = h * TT + l
                    cs = slice(l * P, (l + 1) * P)
                    if n and l:
                        pe.wait_ge(S_["mo_ok"], n)
                    for b in range(3):
                        for hd in range(GH):
                            pe.transpose(side[:, b, hd * P:(hd + 1) * P], cT[:, b * GH + hd, cs], ident[:])
                    pe.wait_ge(S_["g_sb"], n + 1)
                    for hd in range(GH):
                        last = pe.matmul(side[:, 3, hd * P:(hd + 1) * P], arena[:, 11, hd * P:(hd + 1) * P], tri_u[:],
                                         start=True, stop=True)
                    last.then_inc(S_["nat"], 1)
                    pe.wait_ge(S_["kq_n"], 2 * n + 2)
                    for b, src in ((0, 1), (1, 0)):
                        for hd in range(GH):
                            last = pe.transpose(side[:, b, hd * P:(hd + 1) * P], arena[:, src, hd * P:(hd + 1) * P], ident[:])
                    last.then_inc(S_["kqt_tr"], 1)
                    pe.wait_ge(S_["kqt_sb"], 2 * n + 2)
                    pe.wait_ge(S_["vb_ok"], n + 1)
                    pe.wait_ge(S_["em_x"], n + 1)
                    for hd in range(GH):
                        hs = slice(hd * P, (hd + 1) * P)
                        pe.matmul(side[:, 2, hs], arena[:, 7, hs], arena[:, 7, hs], start=True, stop=True)
                        last = pe.matmul(side[:, 3, hs], arena[:, 7, hs], arena[:, 8, hs], start=True, stop=True)
                    last.then_inc(S_["kk"], 1)
                    pe.wait_ge(S_["t1"], n + 1)
                    for hd in range(GH):
                        hs = slice(hd * P, (hd + 1) * P)
                        last = pe.transpose(side[:, 0, hs], arena[:, 9, hs], ident[:])
                    last.then_inc(S_["u_tr"], 1)
                    pe.wait_ge(S_["u_sb"], n + 1)
                    for v in range(len(LEVELS)):
                        m = 6 * n + v
                        pe.wait_ge(S_["as_ok"], m + 1)
                        if v:
                            pe.wait_ge(S_["lt"], m)
                        for hd in range(GH):
                            hs = slice(hd * P, (hd + 1) * P)
                            last = pe.matmul(side[:, 0, hs], arena[:, 12 + v % 2, hs], arena[:, 10, hs], start=True, stop=True)
                        last.then_inc(S_["lx"], 1)
                        pe.wait_ge(S_["lxs"], m + 1)
                        for hd in range(GH):
                            hs = slice(hd * P, (hd + 1) * P)
                            last = pe.matmul(side[:, 1, hs], arena[:, 9, hs], arena[:, 11, hs], start=True, stop=True)
                        last.then_inc(S_["ly"], 1)
                        if v == 0:
                            pe.wait_ge(S_["a_ok"], n + 1)
                        for hd in range(GH):
                            hs = slice(hd * P, (hd + 1) * P)
                            last = pe.matmul(side[:, 2, hs], arena[:, 11, hs], arena[:, 9, hs], start=True, stop=True)
                        last.then_inc(S_["lz"], 1)
                    pe.wait_ge(S_["lt"], 6 * n + 6)
                    pe.wait_ge(S_["qk_ok"], n + 1)
                    if n:
                        pe.wait_ge(S_["st_ok"], n)
                    for hd in range(GH):
                        hs = slice(hd * P, (hd + 1) * P)
                        pe.matmul(side[:, 0, hs], arena[:, 7, hs], state[:, hd, :], start=True, stop=True)
                        last = pe.matmul(side[:, 3, hs], arena[:, 8, hs], state[:, hd, :], start=True, stop=True)
                    last.then_inc(S_["ks"], 1)
                    pe.wait_ge(S_["r_ok"], n + 1)
                    for hd in range(GH):
                        hs = slice(hd * P, (hd + 1) * P)
                        last = pe.matmul(side[:, 1, hs], arena[:, 10, hs], arena[:, 14, hs], start=True, stop=True)
                    last.then_inc(S_["vnew"], 1)
                    pe.wait_ge(S_["vnew_sb"], n + 1)
                    pe.wait_ge(S_["eb_ok"], 4 * n + 4)
                    for hd in range(GH):
                        hs = slice(hd * P, (hd + 1) * P)
                        pe.matmul(side[:, 0, hs], arena[:, 3, hs], arena[:, 15, hs], start=True, stop=True)
                        last = pe.matmul(side[:, 2, hs], arena[:, 6, hs], arena[:, 15, hs], start=True, stop=True)
                    last.then_inc(S_["o_mm"], 1)
                    pe.wait_ge(S_["on_ok"], n + 1)
                    for hd in range(GH):
                        hs = slice(hd * P, (hd + 1) * P)
                        last = pe.transpose(side[:, 1, hs], arena[:, 2, hs], ident[:])
                    last.then_inc(S_["on_tr"], 1)

            def att(h):
                for l in range(TT):
                    if l >= 2:
                        pe.wait_ge(B_["v_ok"], h * TT + l - 1)
                    else:
                        pe.wait_ge(S_["mo_ok"], (h + 1) * TT)
                    for b in range(4):
                        last = pe.transpose(side[:, l % 2, b * P:(b + 1) * P], arena[:, 8 + b, l * P:(l + 1) * P], ident[:])
                    last.then_inc(B_["vt"], 1)
                pe.wait_ge(B_["v_ok"], (h + 1) * TT)
                units = [(hd, i) for hd in range(AH) for i in range(TT)]

                def qk(u):
                    hd, i = units[u]
                    n = h * len(units) + u
                    nk = h * TT + i + 1
                    rows = slice(64 * (hd % 2), 64 * (hd % 2) + 64)
                    sc, _, _ = bank(n)
                    if u >= 2:
                        pe.wait_ge(B_["smax"], n - 1)
                    for hh in range(h + 1):
                        m = min(nk - hh * TT, TT) * P
                        last = pe.matmul(sc[hh][:, 0:m], qbT[rows, hd // 2, i * P:(i + 1) * P],
                                         kb[hh][rows, hd // 2, 0:m], start=True, stop=True)
                    last.then_inc(B_["qk"], 1)

                def pv(u):
                    hd, i = units[u]
                    n = h * len(units) + u
                    nk = h * TT + i + 1
                    _, ptb, ob = bank(n)
                    pbuf = arena[:, 4 + 2 * (n % 2):6 + 2 * (n % 2), :].rearrange("p a (c q) -> p (a c) q", q=P)
                    tbuf = arena[:, 8 + 2 * (n % 2):10 + 2 * (n % 2), :].rearrange("p a (c q) -> p (a c) q", q=P)
                    pe.wait_ge(B_["p_ok"], n + 1)
                    for g in range(h + 1):
                        m = min(nk - g * TT, TT)
                        e = PT_N[h] + (h + 1) * u + g
                        if u >= 2 or g >= 1:
                            pe.wait_ge(B_["pt_ok"], e if g else e - (h + 1))
                        for c in range(m):
                            last = pe.transpose(ptb[:, c * P:(c + 1) * P], pbuf[:, g * TT + c, :], ident[:])
                        last.then_inc(B_["pt"], 1)
                    pe.wait_ge(B_["pt_ok"], PT_N[h] + (h + 1) * (u + 1))
                    if u >= 2:
                        pe.wait_ge(B_["o_ok"], n - 1)
                    for c in range(nk):
                        last = pe.matmul(ob[:, 0:AD], tbuf[:, c, :], vn[c // TT][:, c % TT, hd * AD:(hd + 1) * AD],
                                         start=(c == 0), stop=(c == nk - 1))
                    last.then_inc(B_["pv"], 1)

                qk(0)
                for u in range(len(units)):
                    if u + 1 < len(units):
                        qk(u + 1)
                    pv(u)
                pe.wait_ge(B_["o_ok"], (h + 1) * len(units))
                for b in range(4):
                    if b >= 2:
                        pe.wait_ge(B_["lo"], h * 4 + b - 1)
                    for i in range(TT):
                        last = pe.transpose(side[:, b % 2, i * P:(i + 1) * P], onat[:, i, b * P:(b + 1) * P], ident[:])
                    last.then_inc(B_["tr"], 1)
                pe.wait_ge(B_["lo"], (h + 1) * 4)
                pe.wait_ge(S_["mx_lo"], (h + 1))

            def mem(h):
                units = [(hd, i) for hd in range(MH) for i in range(TT)]

                def qk(u):
                    hd, i = units[u]
                    n = h * len(units) + u
                    if u >= 2:
                        pe.wait_ge(M_["p_ok"], n - 1)
                    for k in range(2):
                        last = pe.matmul(side[:, u % 2, 0:NMEM], qmT[:, 2 * hd + k, i * P:(i + 1) * P], kmT[:, 2 * hd + k, :],
                                         start=(k == 0), stop=(k == 1))
                    last.then_inc(M_["qk"], 1)

                pe.wait_ge(acc_free, MEM_0 + h * MEM_STEPS + KT // 2)
                qk(0)
                for u, (hd, i) in enumerate(units):
                    n = h * len(units) + u
                    if u + 1 < len(units):
                        qk(u + 1)
                    pe.wait_ge(M_["pn"], n + 1)
                    if u >= 2:
                        pe.wait_ge(M_["pt_ok"], n - 1)
                    for c in range(2):
                        last = pe.transpose(side[:, 2 + u % 2, c * P:(c + 1) * P], arena[:, u % 2, c * P:(c + 1) * P], ident[:])
                    last.then_inc(M_["pt"], 1)
                    if i == TT - 1:
                        pe.wait_ge(M_["pt_ok"], n + 1)
                        for d in range(2):
                            o = h * 8 + 2 * hd + d
                            if o % 8 >= 2:
                                pe.wait_ge(M_["lo"], o - 1)
                            for c in range(2):
                                last = pe.matmul(accp[d][0][:], vm[:, c, hd * MD + d * P:hd * MD + (d + 1) * P],
                                                 ptm(hd)[:, c, :], start=(c == 0), stop=(c == 1))
                            last.then_inc(M_["pv"], 1)
                pe.wait_ge(M_["lo"], (h + 1) * 8)

            pe.wait_ge(mask_st, N_CONST)
            u0 = 0
            for h in range(HALVES):
                pre(h)
                u0 = ffn(FFN1_0 + h * FFN_STEPS, u0)
                post(h, FFN1_0 + (h + 1) * FFN_STEPS - 1)
            for h in range(HALVES):
                p0 = MIX_0 + h * MIX_STEPS
                pre(2 + h)
                steps(pe, p0, GDN_STEPS, lambda p, j, par: step(p, par, h_hi, h_lo, KT))
                p = p0 + GDN_STEPS
                step(p, p % 2, h_hi, h_lo, KT, blocks=1)
                gdn(h)
                steps(pe, p + 1, ATT_STEPS, lambda p, j, par: step(p, par, h_hi, h_lo, KT))
                pe.wait_ge(acc_free, p + 1 + ATT_STEPS)
                att(h)
                steps(pe, p + 1 + ATT_STEPS, KT // 2, lambda p, j, par: step(p, par, h_hi, h_lo, KT))
                post(2 + h, p0 + MIX_STEPS - 1)
            pre(4)
            steps(pe, KV_0, KV_STEPS, lambda p, j, par: step(p, par, h_hi[:, :, 0:NMEM], h_lo[:, :, 0:NMEM], KT, NMEM))
            pe.wait_ge(acc_free, MEM_0)
            for c in range(2):
                for k in range(KT):
                    last = pe.transpose(side[:, 2 * c + k // 4, (k % 4) * P:(k % 4 + 1) * P], qmT[:, k, c * P:(c + 1) * P], ident[:])
                last.then_inc(M_["kvt"], 1)
            for h in range(HALVES):
                p0 = MEM_0 + h * MEM_STEPS
                if h == 0:
                    pe.wait_ge(M_["vm"], 2)
                pre(5 + h)
                steps(pe, p0, KT // 2, lambda p, j, par: step(p, par, h_hi, h_lo, KT))
                mem(h)
                steps(pe, p0 + KT // 2, KT // 2, lambda p, j, par: step(p, par, h_hi, h_lo, KT))
                post(4 + h, p0 + MEM_STEPS - 1)
            for h in range(HALVES):
                pre(7 + h)
                u0 = ffn(FFN2_0 + h * FFN_STEPS, u0)
                post(6 + h, FFN2_0 + (h + 1) * FFN_STEPS - 1)

        @block.scalar
        def _(act):
            def prep(p, par):
                if isinstance(p, int) and p >= STEPS:
                    return
                act.wait_ge(w_landed[par], (p // 2 + 1) * 32 if isinstance(p, int) else p * 16 + (32 - 16 * par))
                if not isinstance(p, int) or p >= 2:
                    act.wait_ge(w_used, p - 1)
                act.activation(w_hi[:, par].rearrange("p b k n -> p (b k n)"),
                               w_raw[:, par].rearrange("p b k n -> p (b k n)"), ACT.Copy).then_inc(w_hi_ok, 1)

            def copy2(out, in_, s):
                act.activation(out, in_, ACT.Copy).then_inc(s, 1)

            def pre(q):
                n0, nt = PRE_BASE[q], PRE_TILES[q]
                if q == 4:
                    act.wait_ge(mem_in, 16)
                for k in range(nt):
                    if q < 2:
                        act.wait_ge(x_in, 16 * S // P)
                    elif q != 4:
                        act.wait_ge(post_x, (q - 2 if q < 4 else q - 3) * TT + k + 1)
                    src = memx[:, k, :] if q == 4 else x[:, (TT * (q % 2) if q < 4 else TT * ((q + 1) % 2)) + k, :]
                    if n0 + k:
                        act.wait_ge(pre_ssq, n0 + k)
                    act.activation(pre_junk, src, ACT.Square, accum_out=ssq_pre[:, n0 + k:n0 + k + 1]).then_inc(pre_ssq, 1)
                gi = (0, 0, 1, 1, 4, 2, 2, 3, 3)[q]
                w = nt * P
                for k in range(KT):
                    act.wait_ge(pre_tr, q * KT + k + 1)
                    act.activation(h_hi[:, k, 0:w], side[:, k % 2, 0:w], ACT.Copy, scale=g_pre[:, gi, k:k + 1]).then_inc(pre_hi, 1)

            def post(r):
                for k in range(TT):
                    n = r * TT + k
                    act.wait_ge(post_tr, n + 1)
                    if n:
                        act.wait_ge(post_ssq, n)
                    act.activation(post_junk, side[:, 2 * (k % 2):2 * (k % 2) + 2, :].rearrange("p a n -> p (a n)"),
                                   ACT.Square, accum_out=ssq_post[:, n:n + 1]).then_inc(post_ssq, 1)

            def ffn(p0, u0):
                for c, nf in enumerate(CHUNKS):
                    def up(p, j, par):
                        prep(p + 1, 1 - par)
                        act.wait_ge(w_used, p + 1)
                        act.activation(sg[:, par, :], accp[par][0][:], ACT.Silu).then_inc(act_evac, 1)
                        act.wait_ge(acc_free, p + 1)
                        dst = act_hi[:, j, :] if isinstance(j, int) else act_hi[:, bass.ds(j, 1), :].rearrange("p a n -> p (a n)")
                        act.activation(dst, prod[:, par, :], ACT.Copy).then_inc(act_hi_ok, 1)

                    def down(p, j, par):
                        prep(p + 1, 1 - par)
                        if c == 0:
                            act.wait_ge(w_used, p + 1)
                            dst = oT[:, 2 * j, :] if isinstance(j, int) else oT[:, bass.ds(j * 2, 1), :].rearrange("p a n -> p (a n)")
                            act.activation(dst, accp[par][0][:], ACT.Copy).then_inc(act_evac, 1)
                    steps(act, p0 + FSTEP[c], nf, up)
                    q = p0 + FSTEP[c] + nf
                    if q + KT // 2 >= STEPS:
                        for k in range(KT // 2):
                            down(q + k, k, (q + k) % 2)
                    else:
                        steps(act, q, KT // 2, down)

            def plain(p0, n, dst, cols=TOK):
                def body(p, j, par):
                    prep(p + 1, 1 - par)
                    act.wait_ge(w_used, p + 1)
                    d = dst[:, 2 * j, 0:cols] if isinstance(j, int) else dst[:, bass.ds(j * 2, 1), 0:cols].rearrange("p a n -> p (a n)")
                    act.activation(d, accp[par][0][:, 0:cols], ACT.Copy).then_inc(act_evac, 1)
                steps(act, p0, n, body)

            def mix_in(h):
                p0 = MIX_0 + h * MIX_STEPS
                for j in range(6):
                    p, n = p0 + j, h * 6 + j
                    par = p % 2
                    prep(p + 1, 1 - par)
                    act.wait_ge(w_used, p + 1)
                    raw = rawc(par)
                    act.activation(raw[:, 0, 3:3 + TOK], accp[par][0][:], ACT.Copy)
                    act.activation(raw[:, 1, 3:3 + TOK], accp[par][1][:], ACT.Copy).then_inc(act_evac, 1)
                    act.wait_ge(conv_ok, n + 1)
                    act.activation(cT[:, 2 * j:2 * j + 2, :], yconv, ACT.Silu).then_inc(conv_silu, 1)
                for j in range(2):
                    p = p0 + 6 + j
                    par = p % 2
                    prep(p + 1, 1 - par)
                    act.wait_ge(w_used, p + 1)
                    act.activation(zT[:, 2 * j, :], accp[par][0][:], ACT.Silu)
                    act.activation(zT[:, 2 * j + 1, :], accp[par][1][:], ACT.Silu).then_inc(act_evac, 1)
                p = p0 + GDN_STEPS
                prep(p + 1, 1 - p % 2)
                act.wait_ge(w_used, p + 1)
                act.activation(arena[0:8, 14, :], accp[p % 2][0][0:8, :], ACT.Copy).then_inc(act_evac, 1)

            def gdn(h):
                act.wait_ge(S_["ab_tr"], h + 1)
                act.activation(sm[:, 16:18, :].rearrange("p a n -> p (a n)"), side[:, 0, 0:32], ACT.Copy).then_inc(S_["ab_sb"], 1)
                act.wait_ge(S_["ab_exp"], 2 * h + 1)
                act.activation(sm[:, 3, :], sm[:, 3, :], ACT.Exp)
                act.activation(sm[:, 2, :], sm[:, 2, :], ACT.Exp).then_inc(S_["ab_exp"], 1)
                act.wait_ge(S_["g_e"], 2 * h + 1)
                act.activation(sm[:, 4, :], sm[:, 7, :], ACT.Exp)
                act.activation(sm[:, 5, :], sm[:, 8, :], ACT.Exp)
                act.activation(sm[:, 6, :], sm[:, 9, :], ACT.Exp).then_inc(S_["g_e"], 1)
                for l in range(TT):
                    n = h * TT + l
                    act.wait_ge(S_["nat"], n + 1)
                    act.activation(arena[:, 4, :], side[:, 0, :], ACT.Square).then_inc(S_["sq"], 1)
                    act.activation(arena[:, 5, :], side[:, 1, :], ACT.Square).then_inc(S_["sq"], 1)
                    act.wait_ge(S_["em_x"], n + 1)
                    act.activation(arena[:, 4, :], arena[:, 12, :], ACT.Exp).then_inc(S_["e_ok"], 1)
                    act.wait_ge(S_["kqt_tr"], n + 1)
                    copy2(arena[:, 7, :], side[:, 0, :], S_["kqt_sb"])
                    copy2(arena[:, 8, :], side[:, 1, :], S_["kqt_sb"])
                    act.wait_ge(S_["u_tr"], n + 1)
                    copy2(arena[:, 10, :], side[:, 0, :], S_["u_sb"])
                    for v in range(len(LEVELS)):
                        m = 6 * n + v
                        act.wait_ge(S_["lx"], m + 1)
                        copy2(arena[:, 11, :], side[:, 0, :], S_["lxs"])
                    act.wait_ge(S_["vnew"], n + 1)
                    copy2(arena[:, 15, :], side[:, 1, :], S_["vnew_sb"])
                    act.wait_ge(S_["o_ok"], n + 1)
                    act.activation(arena[:, 4, :], arena[:, 0, :], ACT.Square).then_inc(S_["o_sq"], 1)

            def att(h):
                act.wait_ge(S_["mo_ok"], (h + 1) * TT)
                act.activation(h_hi[:, 0:4, :], zT[:], ACT.Copy).then_inc(S_["mx_hi"], 1)
                for l in range(TT):
                    act.wait_ge(B_["vt"], h * TT + l + 1)
                    copy2(vn[h][:, l, :], side[:, l % 2, :], B_["v_ok"])
                n_units = AH * TT
                for u in range(n_units):
                    n = h * n_units + u
                    i = u % TT
                    nk = h * TT + i + 1
                    pb = arena[:, 4 + 2 * (n % 2):6 + 2 * (n % 2), :].rearrange("p a n -> p (a n)")
                    act.wait_ge(B_["nmx"], n + 1)
                    act.activation(pb[:, 0:nk * P], pb[:, 0:nk * P], ACT.Exp, bias=sm[:, 19, n % 2:n % 2 + 1], scale=AD ** -0.5,
                                   accum_out=sm[:, 20, n % 2:n % 2 + 1]).then_inc(B_["p_ok"], 1)
                    tb = arena[:, 8 + 2 * (n % 2):10 + 2 * (n % 2), :]
                    _, ptb, _ = bank(n)
                    for g in range(h + 1):
                        m = min(nk - g * TT, TT) * P
                        act.wait_ge(B_["pt"], PT_N[h] + (h + 1) * u + g + 1)
                        copy2(tb[:, g, 0:m], ptb[:, 0:m], B_["pt_ok"])
                for b in range(4):
                    act.wait_ge(B_["tr"], h * 4 + b + 1)
                    act.activation(h_hi[:, 4 + b, :], side[:, b % 2, :], ACT.Copy).then_inc(B_["hi"], 1)

            def mem(h):
                n_units = MH * TT
                for u in range(n_units):
                    n = h * n_units + u
                    hd, i = u // TT, u % TT
                    act.wait_ge(M_["nmx"], n + 1)
                    act.activation(arena[:, u % 2, 0:NMEM], side[:, u % 2, 0:NMEM], ACT.Exp, bias=sm[:, 19, n % 2:n % 2 + 1],
                                   scale=MD ** -0.5, accum_out=sm[:, 20, n % 2:n % 2 + 1]).then_inc(M_["p_ok"], 1)
                    act.wait_ge(M_["pt"], n + 1)
                    act.activation(ptm(hd)[:, :, i * P:(i + 1) * P], side[:, 2 + u % 2, 0:NMEM].rearrange("p (c q) -> p c q", c=2),
                                   ACT.Copy).then_inc(M_["pt_ok"], 1)
                    if i == TT - 1:
                        for d in range(2):
                            o = h * 8 + 2 * hd + d
                            act.wait_ge(M_["pv"], o + 1)
                            act.activation(h_hi[:, 2 * hd + d, :], accp[d][0][:], ACT.Copy).then_inc(M_["hi"], 1)

            act.wait_ge(const_in, 16 * N_SMALL)
            act.activation(neg_a[:], neg_a[:], ACT.Exp).then_inc(neg_rdy, 1)
            prep(0, 0)
            for h in range(HALVES):
                pre(h)
                ffn(FFN1_0 + h * FFN_STEPS, 0)
                post(h)
            for h in range(HALVES):
                p0 = MIX_0 + h * MIX_STEPS
                pre(2 + h)
                mix_in(h)
                gdn(h)
                p = p0 + GDN_STEPS + 1
                plain(p, 2, qbT)
                plain(p + 2, 2, kb[h])
                plain(p + 4, 2, arena[:, 8:12, :])
                att(h)
                plain(p + ATT_STEPS, KT // 2, oT)
                post(2 + h)
            pre(4)
            plain(KV_0, KT // 2, kmT, NMEM)
            plain(KV_0 + KT // 2, KT // 2, qmT, NMEM)
            for h in range(HALVES):
                p0 = MEM_0 + h * MEM_STEPS
                if h == 0:
                    for c in range(2):
                        act.wait_ge(M_["kvt"], c + 1)
                        copy2(vm[:, c, :], side[:, 2 * c:2 * c + 2, :].rearrange("p a n -> p (a n)"), M_["vm"])
                pre(5 + h)
                plain(p0, KT // 2, qmT)
                mem(h)
                plain(p0 + KT // 2, KT // 2, oT)
                post(4 + h)
            for h in range(HALVES):
                pre(7 + h)
                ffn(FFN2_0 + h * FFN_STEPS, 0)
                post(6 + h)

        @block.vector
        def _(dve):
            n_seq = [0]

            def link(ins):
                n_seq[0] += 1
                ins.then_inc(dve_seq, 1)
                dve.wait_ge(dve_seq, n_seq[0])

            def prep(p, par):
                if isinstance(p, int) and p >= STEPS:
                    return
                dve.wait_ge(w_hi_ok, p + 1)
                dve.tensor_tensor(w_lo[:, par].rearrange("p b k n -> p (b k n)"),
                                  w_raw[:, par].rearrange("p b k n -> p (b k n)"),
                                  w_hi[:, par].bitcast(F32).rearrange("p b k n -> p (b k n)"),
                                  ALU.subtract).then_inc(w_lo_ok, 1)

            def lo_of(out, src, hi, s):
                dve.tensor_tensor(out, src, hi.bitcast(F32), ALU.subtract).then_inc(s, 1)

            def pre(q):
                n0, nt = PRE_BASE[q], PRE_TILES[q]
                if q:
                    dve.wait_ge(post_x, (q if q <= 4 else q - 1) * TT)
                dve.wait_ge(pre_rs, q + 1)
                for k in range(nt):
                    src = memx[:, k, :] if q == 4 else x[:, (TT * (q % 2) if q < 4 else TT * ((q + 1) % 2)) + k, :]
                    dve.tensor_scalar(xn[:, k, :], src, rs_pre[:, n0 + k:n0 + k + 1], None, ALU.mult).then_inc(pre_xn, 1)
                gi = (0, 0, 1, 1, 4, 2, 2, 3, 3)[q]
                w = nt * P
                for k in range(KT):
                    dve.wait_ge(pre_hi, q * KT + k + 1)
                    dve.scalar_tensor_tensor(out=h_lo[:, k, 0:w], in0=side[:, k % 2, 0:w], scalar=g_pre[:, gi, k:k + 1],
                                             in1=h_hi[:, k, 0:w].bitcast(F32), op0=ALU.mult, op1=ALU.subtract).then_inc(pre_lo, 1)

            def post(r):
                dve.wait_ge(grow_in, 16 * (r + 1))
                for k in range(TT):
                    n = r * TT + k
                    xt = x[:, (r % 2) * TT + k, :]
                    dve.wait_ge(post_rs, n + 1)
                    if n:
                        dve.wait_ge(post_x, n)
                    link(dve.scalar_tensor_tensor(out=post_tmp, in0=side[:, 2 * (k % 2):2 * (k % 2) + 2, :].rearrange("p a n -> p (a n)"),
                                                  scalar=rs_post[:, n:n + 1], in1=g_row, op0=ALU.mult, op1=ALU.mult))
                    dve.scalar_tensor_tensor(out=xt, in0=post_tmp, scalar=0.5 if r // 2 in (0, 3) else 1.0, in1=xt,
                                             op0=ALU.mult, op1=ALU.add).then_inc(post_x, 1)

            def ffn(p0, skip, h, u0):
                for c, nf in enumerate(CHUNKS):
                    sk = ffn_skip(skip, h, c)

                    def up(p, j, par):
                        prep(p + 1, 1 - par)
                        dve.wait_ge(act_evac, p + (1 - sk))
                        dve.tensor_tensor(prod[:, par, :], accp[par][1][:], sg[:, par, :], ALU.mult).then_inc(acc_free, 1)
                        dve.wait_ge(act_hi_ok, j + (u0 + 1))
                        dst = act_lo[:, j, :] if isinstance(j, int) else act_lo[:, bass.ds(j, 1), :].rearrange("p a n -> p (a n)")
                        hi = act_hi[:, j, :] if isinstance(j, int) else act_hi[:, bass.ds(j, 1), :].rearrange("p a n -> p (a n)")
                        dve.tensor_tensor(dst, prod[:, par, :], hi.bitcast(F32), ALU.subtract).then_inc(act_lo_ok, 1)

                    def down(p, j, par):
                        prep(p + 1, 1 - par)
                        dve.wait_ge(w_used, p + 1)

                        def ot(k):
                            return oT[:, 2 * j + k, :] if isinstance(j, int) else oT[:, bass.ds(j * 2 + k, 1), :].rearrange("p a n -> p (a n)")
                        if c == 0:
                            dve.wait_ge(act_evac, p + (1 - sk))
                            dve.tensor_copy(ot(1), accp[par][1][:]).then_inc(acc_free, 1)
                        else:
                            dve.tensor_tensor(ot(0), accp[par][0][:], ot(0), ALU.add)
                            dve.tensor_tensor(ot(1), accp[par][1][:], ot(1), ALU.add).then_inc(acc_free, 1)
                    steps(dve, p0 + FSTEP[c], nf, up)
                    u0 += nf
                    q = p0 + FSTEP[c] + nf
                    if q + KT // 2 >= STEPS:
                        for k in range(KT // 2):
                            down(q + k, k, (q + k) % 2)
                    else:
                        steps(dve, q, KT // 2, down)
                return u0

            def plain(p0, n, dst, cols=TOK):
                def body(p, j, par):
                    prep(p + 1, 1 - par)
                    dve.wait_ge(act_evac, p + (1 - MID_SKIP))
                    d = dst[:, 2 * j + 1, 0:cols] if isinstance(j, int) else dst[:, bass.ds(j * 2 + 1, 1), 0:cols].rearrange("p a n -> p (a n)")
                    dve.tensor_copy(d, accp[par][1][:, 0:cols]).then_inc(acc_free, 1)
                steps(dve, p0, n, body)

            def mix_in(h):
                p0 = MIX_0 + h * MIX_STEPS
                for j in range(6):
                    p, n = p0 + j, h * 6 + j
                    par = p % 2
                    prep(p + 1, 1 - par)
                    raw = rawc(par)
                    ct = slice(2 * j, 2 * j + 2)
                    if n:
                        dve.wait_ge(conv_ok, n)
                    link(dve.tensor_copy(raw[:, :, 0:3], carry[:, ct, :]))
                    dve.wait_ge(act_evac, p + 1 - MID_SKIP)
                    dve.tensor_copy(carry[:, ct, :], raw[:, :, TOK:TOK + 3]).then_inc(acc_free, 1)
                    dve.wait_ge(acc_free, p + 1)
                    if n:
                        dve.wait_ge(conv_silu, n)
                    for tap in range(4):
                        for b in range(2):
                            w = conv_w[:, 2 * j + b, tap:tap + 1]
                            if tap == 0:
                                i = dve.tensor_scalar(yconv[:, b, :], raw[:, b, 0:TOK], w, None, ALU.mult)
                            else:
                                i = dve.scalar_tensor_tensor(out=yconv[:, b, :], in0=raw[:, b, tap:tap + TOK], scalar=w,
                                                             in1=yconv[:, b, :], op0=ALU.mult, op1=ALU.add)
                            if b == 1 and tap < 3:
                                link(i)
                    i.then_inc(conv_ok, 1)
                for j in range(2):
                    p = p0 + 6 + j
                    prep(p + 1, 1 - p % 2)
                    dve.wait_ge(act_evac, p + 1 - MID_SKIP)
                    dve.tensor_scalar(zT[:, 2 * j:2 * j + 2, :], zT[:, 2 * j:2 * j + 2, :], ngain[:], None, ALU.mult).then_inc(acc_free, 1)
                p = p0 + GDN_STEPS
                prep(p + 1, 1 - p % 2)
                dve.wait_ge(act_evac, p + 1 - MID_SKIP)
                dve.tensor_copy(arena[0:8, 15, :], arena[0:8, 14, :]).then_inc(acc_free, 1)

            def hv(i):
                return arena[:, i, :].rearrange("p (h c) -> p h c", h=GH)

            def sv(b):
                return side[:, b, :].rearrange("p (h c) -> p h c", h=GH)

            def gdn(h):
                c4 = lambda v: v.rearrange("p (l h) -> p l h", h=GH)
                dtb = dt_row[:].unsqueeze(1).to_broadcast([P, TT, GH])
                nab = neg_a[:].unsqueeze(1).to_broadcast([P, TT, GH])
                ab = sm[:, 16:18, :].rearrange("p a n -> p (a n)").rearrange("p (l e) -> p l e", e=8)
                g, be, eb, u = sm[:, 0, :], sm[:, 1, :], sm[:, 2, :], sm[:, 3, :]
                xx, q, z, z2 = sm[:, 7, :], sm[:, 8, :], sm[:, 9, :], sm[:, 11, :]
                dve.wait_ge(S_["ab_sb"], h + 1)
                link(dve.tensor_tensor(c4(xx), ab[:, :, 0:GH], dtb, ALU.add))
                link(dve.tensor_scalar(c4(eb), ab[:, :, GH:2 * GH], -1.0, 80.0, ALU.mult, ALU.min))
                dve.scalar_tensor_tensor(out=u, in0=xx, scalar=-1.0, in1=xx, op0=ALU.mult, op1=ALU.min).then_inc(S_["ab_exp"], 1)
                dve.wait_ge(S_["ab_exp"], 2 * h + 2)
                link(dve.tensor_scalar(eb, eb, 1.0, None, ALU.add))
                link(dve.reciprocal(be, eb))
                link(dve.tensor_scalar(q, u, 2.0, None, ALU.add))
                link(dve.reciprocal(z2, q))
                link(dve.tensor_tensor(z, u, z2, ALU.mult))
                link(dve.tensor_tensor(z2, z, z, ALU.mult))
                link(dve.tensor_scalar(q, z2, 1.0 / 15, None, ALU.mult))
                for odd in (13, 11, 9, 7, 5, 3):
                    link(dve.scalar_tensor_tensor(out=q, in0=q, scalar=1.0 / odd, in1=z2, op0=ALU.add, op1=ALU.mult))
                link(dve.scalar_tensor_tensor(out=q, in0=q, scalar=1.0, in1=z, op0=ALU.add, op1=ALU.mult))
                link(dve.tensor_scalar(xx, xx, 0.0, None, ALU.max))
                link(dve.scalar_tensor_tensor(out=q, in0=q, scalar=2.0, in1=xx, op0=ALU.mult, op1=ALU.add))
                dve.wait_ge(neg_rdy, 1)
                link(dve.tensor_tensor(c4(q), c4(q), nab, ALU.mult))
                dve.tensor_scalar(g, q, -1.0, None, ALU.mult).then_inc(S_["g_ok"], 1)
                dve.wait_ge(S_["g_mm"], h + 1)
                link(dve.tensor_copy(sm[:, 7, :], side[:, 1, 0:16]))
                link(dve.tensor_copy(sm[:, 8, :], side[:, 2, 0:16]))
                dve.tensor_tensor(sm[:, 9, :], sm[:, 8, :], sm[:, 7, :], ALU.subtract).then_inc(S_["g_e"], 1)
                dve.wait_ge(S_["g_e"], 2 * h + 2)
                dve.tensor_tensor(sm[:, 15, :], sm[:, 4, :], be, ALU.mult).then_inc(S_["g_be"], 1)
                for l in range(TT):
                    n = h * TT + l
                    cs = slice(l * 4, l * 4 + 4)
                    if l:
                        dve.wait_ge(S_["lz"], 6 * n)
                    dve.tensor_copy(hv(11), bc_h(g[:, cs])).then_inc(S_["g_sb"], 1)
                    dve.wait_ge(S_["sq"], 2 * n + 1)
                    dve.tensor_reduce(sm[:, 10, 0:4], hv(4), AXX, ALU.add).then_inc(S_["ssr"], 1)
                    dve.wait_ge(S_["sq"], 2 * n + 2)
                    dve.tensor_reduce(sm[:, 10, 4:8], hv(5), AXX, ALU.add).then_inc(S_["ssr"], 1)
                    link(dve.tensor_tensor(hv(12), sv(3), bc_h(sm[:, 7, cs]), ALU.subtract))
                    dve.scalar_tensor_tensor(out=arena[:, 12, :], in0=arena[:, 12, :], scalar=-1.0, in1=arena[:, 12, :],
                                             op0=ALU.mult, op1=ALU.min).then_inc(S_["em_x"], 1)
                    dve.tensor_tensor(hv(2), sv(2), bc_h(be[:, cs]), ALU.mult).then_inc(S_["vb_ok"], 1)
                    dve.wait_ge(S_["rs2"], n + 1)
                    dve.tensor_tensor(hv(0), sv(0), bc_h(sm[:, 13, 0:4]), ALU.mult).then_inc(S_["kq_n"], 1)
                    dve.tensor_tensor(hv(1), sv(1), bc_h(sm[:, 13, 4:8]), ALU.mult).then_inc(S_["kq_n"], 1)
                    dve.wait_ge(S_["kk"], n + 1)
                    dve.wait_ge(S_["eb_ok"], 4 * n + 3)
                    dve.tensor_tensor(hv(5), sv(2), hv(5), ALU.mult).then_inc(S_["a_ok"], 1)
                    dve.tensor_tensor(hv(6), sv(3), hv(6), ALU.mult).then_inc(S_["qk_ok"], 1)
                    dve.wait_ge(S_["a_ok"], n + 1)
                    link(dve.tensor_tensor(hv(9), hv(5), bc_m(m_lvl[:, 0, :]), ALU.mult))
                    dve.tensor_tensor(hv(9), bc_m(ident[:]), hv(9), ALU.subtract).then_inc(S_["t1"], 1)
                    for v in range(len(LEVELS)):
                        m = 6 * n + v
                        dve.wait_ge(S_["ly"], m + 1)
                        dve.tensor_tensor(hv(10), hv(10), sv(1), ALU.subtract).then_inc(S_["lu"], 1)
                        dve.wait_ge(S_["lz"], m + 1)
                        dve.tensor_tensor(hv(9), hv(9), sv(2), ALU.subtract).then_inc(S_["lt"], 1)
                    dve.wait_ge(S_["ks"], n + 1)
                    link(dve.tensor_tensor(hv(14), sv(0), bc_h(sm[:, 15, cs]), ALU.mult))
                    dve.tensor_tensor(hv(14), hv(2), hv(14), ALU.subtract).then_inc(S_["r_ok"], 1)
                    link(dve.tensor_tensor(hv(0), sv(3), bc_h(sm[:, 4, cs]), ALU.mult))
                    dve.wait_ge(S_["o_mm"], n + 1)
                    dve.wait_ge(S_["s_scl"], n + 1)
                    dve.tensor_tensor(state[:], state[:], sv(0), ALU.add).then_inc(S_["st_ok"], 1)
                    dve.tensor_tensor(hv(0), hv(0), sv(2), ALU.add).then_inc(S_["o_ok"], 1)
                    dve.wait_ge(S_["o_sq"], n + 1)
                    dve.tensor_reduce(sm[:, 14, 4:8], hv(4), AXX, ALU.add).then_inc(S_["o_ssr"], 1)
                    dve.wait_ge(S_["o_rs"], n + 1)
                    dve.tensor_tensor(hv(2), hv(0), bc_h(sm[:, 14, 8:12]), ALU.mult).then_inc(S_["on_ok"], 1)
                    dve.wait_ge(S_["on_tr"], n + 1)
                    dve.tensor_tensor(zT[:, :, l * P:(l + 1) * P], sv(1), zT[:, :, l * P:(l + 1) * P], ALU.mult).then_inc(S_["mo_ok"], 1)

            def log_counts(h):
                dd = arena[:, 0:2, :].rearrange("p a n -> p (a n)")
                m4 = arena[:, 2:4, :].rearrange("p a n -> p (a n)")
                m16 = arena[:, 4:6, :].rearrange("p a n -> p (a n)")
                lm = arena[:, 12:14, :].rearrange("p a n -> p (a n)")
                di = dd.bitcast(I32)
                ti = lm.bitcast(I32)
                link(dve.tensor_scalar(ti, di, 3, None, ALU.bitwise_and))
                link(dve.tensor_scalar(m4, ti, 0.0, None, ALU.is_equal))
                link(dve.tensor_scalar(ti, di, 15, None, ALU.bitwise_and))
                link(dve.tensor_scalar(m16, ti, 0.0, None, ALU.is_equal))
                link(dve.scalar_tensor_tensor(out=m4, in0=di, scalar=512.0, in1=m4, op0=ALU.is_le, op1=ALU.mult))
                link(dve.tensor_tensor(m4, m4, m16, ALU.add))
                link(dve.scalar_tensor_tensor(out=m4, in0=di, scalar=128.0, in1=m4, op0=ALU.is_le, op1=ALU.add))
                link(dve.scalar_tensor_tensor(out=m4, in0=di, scalar=0.0, in1=m4, op0=ALU.is_ge, op1=ALU.mult))
                link(dve.tensor_scalar(lm, m4, 2.0, 8 * math.log(2.0), ALU.is_ge, ALU.mult))
                link(dve.tensor_scalar(m16, m4, 3.0, 8 * math.log(1.5), ALU.is_ge, ALU.mult))
                link(dve.tensor_tensor(lm, lm, m16, ALU.add))
                link(dve.tensor_scalar(m4, m4, 1.0, NEG, ALU.is_lt, ALU.mult))
                dve.tensor_tensor(lm, lm, m4, ALU.add).then_inc(B_["lm"], 1)

            def att(h):
                n_units = AH * TT
                dve.wait_ge(S_["o_sq"], (h + 1) * TT)
                dve.wait_ge(S_["mx_hi"], h + 1)
                lo_of(h_lo[:, 0:4, :], zT[:], h_hi[:, 0:4, :], S_["mx_lo"])
                dve.wait_ge(B_["di"], h + 1)
                log_counts(h)
                for u in range(n_units):
                    n = h * n_units + u
                    hd, i = u // TT, u % TT
                    nk = h * TT + i + 1
                    sc, ptb, ob = bank(n)
                    sbuf = arena[:, 4 + 2 * (n % 2):6 + 2 * (n % 2), :].rearrange("p a n -> p (a n)")
                    bias = arena[:, 2 * (hd % 2):2 * (hd % 2) + 2, :].rearrange("p a n -> p (a n)")
                    b0 = S - nk * P
                    dve.wait_ge(B_["bias_i"], 3 * (h * AH + hd) + 3)
                    dve.wait_ge(B_["qk"], n + 1)
                    if u >= 2:
                        dve.wait_ge(B_["pt"], PT_N[h] + (h + 1) * (u - 1))
                    for hh in range(h + 1):
                        m = min(nk - hh * TT, TT) * P
                        i_ = dve.tensor_tensor_reduce(sbuf[:, hh * TOK:hh * TOK + m], sc[hh][:, 0:m],
                                                      bias[:, b0 + hh * TOK:b0 + hh * TOK + m], 1.0, NEG, ALU.add, ALU.max,
                                                      sm[:, 18, 2 * (n % 2) + hh:2 * (n % 2) + hh + 1])
                    i_.then_inc(B_["smax"], 1)
                    dve.wait_ge(B_["smax"], n + 1)
                    mx = sm[:, 18, 2 * (n % 2):2 * (n % 2) + 1]
                    if h:
                        link(dve.tensor_tensor(mx, mx, sm[:, 18, 2 * (n % 2) + 1:2 * (n % 2) + 2], ALU.max))
                    dve.tensor_scalar(sm[:, 19, n % 2:n % 2 + 1], mx, -(AD ** -0.5), None, ALU.mult).then_inc(B_["nmx"], 1)

                    def fin(u):
                        n = h * n_units + u
                        hd, i = u // TT, u % TT
                        dve.wait_ge(B_["p_ok"], n + 1)
                        link(dve.reciprocal(sm[:, 22, n % 2:n % 2 + 1], sm[:, 20, n % 2:n % 2 + 1]))
                        dve.wait_ge(B_["pv"], n + 1)
                        dve.tensor_scalar(onat[:, i, hd * AD:(hd + 1) * AD], bank(n)[2][:, 0:AD], sm[:, 22, n % 2:n % 2 + 1],
                                          None, ALU.mult).then_inc(B_["o_ok"], 1)
                    if u >= 1:
                        fin(u - 1)
                fin(n_units - 1)
                for b in range(4):
                    dve.wait_ge(B_["hi"], h * 4 + b + 1)
                    lo_of(h_lo[:, 4 + b, :], side[:, b % 2, :], h_hi[:, 4 + b, :], B_["lo"])

            def mem(h):
                n_units = MH * TT
                for u in range(n_units):
                    n = h * n_units + u
                    hd, i = u // TT, u % TT

                    def mx(u):
                        n = h * n_units + u
                        dve.wait_ge(M_["qk"], n + 1)
                        link(dve.tensor_reduce(sm[:, 18, n % 2:n % 2 + 1], side[:, u % 2, 0:NMEM], AXX, ALU.max))
                        dve.tensor_scalar(sm[:, 19, n % 2:n % 2 + 1], sm[:, 18, n % 2:n % 2 + 1], -(MD ** -0.5), None, ALU.mult).then_inc(M_["nmx"], 1)
                    if u == 0:
                        mx(0)
                    dve.wait_ge(M_["p_ok"], n + 1)
                    if u + 1 < n_units:
                        mx(u + 1)
                    link(dve.reciprocal(sm[:, 22, n % 2:n % 2 + 1], sm[:, 20, n % 2:n % 2 + 1]))
                    dve.tensor_scalar(arena[:, u % 2, 0:NMEM], arena[:, u % 2, 0:NMEM], sm[:, 22, n % 2:n % 2 + 1], None, ALU.mult).then_inc(M_["pn"], 1)
                    if i == TT - 1:
                        for d in range(2):
                            o = h * 8 + 2 * hd + d
                            dve.wait_ge(M_["hi"], o + 1)
                            lo_of(h_lo[:, 2 * hd + d, :], accp[d][0][:], h_hi[:, 2 * hd + d, :], M_["lo"])

            dve.wait_ge(mask_st, N_CONST)
            prep(0, 0)
            u0 = 0
            for h in range(HALVES):
                pre(h)
                u0 = ffn(FFN1_0 + h * FFN_STEPS, FFN1_SKIP, h, u0)
                post(h)
            for h in range(HALVES):
                p = MIX_0 + h * MIX_STEPS + GDN_STEPS + 1
                pre(2 + h)
                mix_in(h)
                gdn(h)
                plain(p, 2, qbT)
                plain(p + 2, 2, kb[h])
                plain(p + 4, 2, arena[:, 8:12, :])
                att(h)
                plain(p + ATT_STEPS, KT // 2, oT)
                post(2 + h)
            pre(4)
            plain(KV_0, KT // 2, kmT, NMEM)
            plain(KV_0 + KT // 2, KT // 2, qmT, NMEM)
            for h in range(HALVES):
                p0 = MEM_0 + h * MEM_STEPS
                pre(5 + h)
                plain(p0, KT // 2, qmT)
                mem(h)
                plain(p0 + KT // 2, KT // 2, oT)
                post(4 + h)
            for h in range(HALVES):
                pre(7 + h)
                u0 = ffn(FFN2_0 + h * FFN_STEPS, FFN2_SKIP, h, u0)
                post(6 + h)


_INS = ["x", "mem", "ffn1_pre_g", "ffn1_w_gate", "ffn1_w_up", "ffn1_w_down", "ffn1_post_g",
        "mix_pre_g", "w_in", "gdn_conv_w", "gdn_a_log", "gdn_dt_bias", "gdn_norm_g", "w_out", "mix_post_g",
        "mem_pre_g", "mem_kv_g", "mem_wq", "mem_wk", "mem_wv", "mem_wo", "mem_post_g",
        "ffn2_pre_g", "ffn2_w_gate", "ffn2_w_up", "ffn2_w_down", "ffn2_post_g"]


def kernel(**inputs):
    import numpy as np
    import concourse.bacc as bacc
    from concourse.bass_utils import run_bass_kernel_spmd

    nc = bacc.Bacc("TRN2", target_bir_lowering=False, num_devices=1)
    arrays, aps = {}, {}
    for name in _INS:
        a = np.ascontiguousarray(inputs[name])
        arrays["in_" + name] = a
        aps[name] = nc.dram_tensor("in_" + name, a.shape, mybir.dt.from_np(a.dtype), kind="ExternalInput").ap()
    aps["out"] = nc.dram_tensor("out_x", (1, S, D), F32, kind="ExternalOutput").ap()
    with nc.allow_non_contiguous_dma(reason="small gains, channels onto partitions"):
        hybrid_layer(nc, aps)
    got = run_bass_kernel_spmd(nc, [arrays], core_ids=[0])
    return got.results[0]["out_x"]
```

```python
from contextlib import ExitStack
import math

import concourse.bass as bass
from concourse import mybir

F32 = mybir.dt.float32
F32R = mybir.dt.float32r
I32 = mybir.dt.int32
ACT = mybir.ActivationFunctionType
ALU = mybir.AluOpType
AXX = mybir.AxisListType.X

P = 128
D = 1024
S = 1024
NMEM = 256
DFF = 2816
KT = D // P
TOK = 512
HALVES = S // TOK
TT = TOK // P
FT = DFF // P
CHUNKS = (8, 7, 7)
assert sum(CHUNKS) == FT
EPS = 1e-6

GH, GD = 4, 128
AH, AD = 8, 64
GW = GH * GD
AB0 = 4 * GW
QB0 = AB0 + 2 * GH
LEVELS = (2, 4, 8, 16, 32, 64)
MH, MD = 4, 256
NEG = -1.0e30

FFN_STEPS = sum(CHUNKS) + len(CHUNKS) * (KT // 2)
GDN_STEPS = 2 * GW * 4 // (2 * P) // 2
ATT_STEPS = 3 * AH * AD // (2 * P)
MIX_STEPS = GDN_STEPS + 1 + ATT_STEPS + KT // 2
KV_STEPS = KT
MEM_STEPS = KT
FFN1_0 = 0
MIX_0 = FFN1_0 + HALVES * FFN_STEPS
KV_0 = MIX_0 + HALVES * MIX_STEPS
MEM_0 = KV_0 + KV_STEPS
FFN2_0 = MEM_0 + HALVES * MEM_STEPS
STEPS = FFN2_0 + HALVES * FFN_STEPS

PRE_TILES = (4, 4, 4, 4, 2, 4, 4, 4, 4)
PRE_BASE = [sum(PRE_TILES[:i]) for i in range(len(PRE_TILES))]
POSTS_BEFORE = (0, 0, 1, 2, 3, 4, 4, 5, 6)

N_SMALL = 12
N_IDENT = 4
N_CONST = 8 + 3 * (1 + len(LEVELS))
PT_N = (0, AH * TT)


def hybrid_layer(nc, t):
    ctx = ExitStack()
    with ctx:
        def sb(name, shape, dt=F32, scope=ctx):
            return scope.enter_context(nc.sbuf_tensor(name, shape, dt))

        def sem(name):
            return ctx.enter_context(nc.semaphore(name))

        x = sb("x", [P, S // P, D])
        w_raw = sb("w_raw", [P, 2, 2, KT, P])
        w_hi = sb("w_hi", [P, 2, 2, KT, P], F32R)
        w_lo = sb("w_lo", [P, 2, 2, KT, P], F32R)
        h_hi = sb("h_hi", [P, KT, TOK], F32R)
        h_lo = sb("h_lo", [P, KT, TOK], F32R)
        arena = sb("arena", [P, 16, 512])
        xn = arena[:, 0:8, :].rearrange("p (t c) n -> p t (c n)", t=TT)
        oT = arena[:, 8:16, :]
        ident = sb("ident", [P, P])
        ones = sb("ones", [P, P])
        tri_u = sb("tri_u", [P, P])
        tri_s = sb("tri_s", [P, P])
        m_lvl = sb("m_lvl", [P, 1 + len(LEVELS), P])

        g_pre = sb("g_pre", [P, 5, KT])
        conv_w = sb("conv_w", [P, 12, 4])
        carry = sb("carry", [P, 12, 3])
        ngain = sb("ngain", [P, 1])
        dt_row = sb("dt_row", [P, GH])
        neg_a = sb("neg_a", [P, GH])
        state = sb("state", [P, GH, GD])
        yconv = arena[:, 6:8, :]
        ssq_pre = sb("ssq_pre", [P, 34])
        rs_pre = sb("rs_pre", [P, 34])
        ssq_post = sb("ssq_post", [P, 32])
        rs_post = sb("rs_post", [P, 32])
        half_pow = sb("half_pow", [P, 8])
        sm = sb("sm", [P, 24, 16])

        def scoped(specs):
            with ExitStack() as s:
                return [sb(n, sh, dt, s) for n, sh, dt in specs]

        act_hi, act_lo, sg, prod = scoped([
            ("act_hi", [P, 8, TOK], F32R), ("act_lo", [P, 8, TOK], F32R),
            ("sg", [P, 2, TOK], F32), ("prod", [P, 2, TOK], F32)])
        cT, zT, kb0, vn0 = scoped([
            ("cT", [P, 12, TOK], F32), ("zT", [P, GH, TOK], F32),
            ("kb0", [P, 4, TOK], F32), ("vn0", [P, TT, TOK], F32)])
        qmT, kmT, vm, memx = scoped([
            ("qmT", [P, KT, TOK], F32), ("kmT", [P, KT, NMEM], F32),
            ("vm", [P, 2, D], F32), ("memx", [P, 2, D], F32)])
        kb1, vn1, qbT = cT[:, 0:4, :], cT[:, 4:8, :], cT[:, 8:12, :]
        kb = (kb0, kb1)
        vn = (vn0, vn1)

        def post_bufs(r):
            places = {1: (vn0[:, 0:2, :], vn0[:, 2:4, :], kb0[:, 0:2, :]),
                      2: (cT[:, 10:12, :], zT[:, 0:2, :], zT[:, 2:4, :]),
                      3: (vn0[:, 0:2, :], vn0[:, 2:4, :], arena[:, 4:6, :])}
            got = places.get(r, (arena[:, 6:8, :], arena[:, 2:4, :], arena[:, 0:2, :]))
            return [v.rearrange("p a n -> p (a n)") for v in got]
        onat = zT

        def rawc(par):
            return arena[:, 0:8, :].rearrange("p a n -> p (a n)")[:, par * 2 * (TOK + 3):(par + 1) * 2 * (TOK + 3)].rearrange(
                "p (b n) -> p b n", b=2)

        def ptm(hd):
            return arena[:, 4 + 2 * (hd % 2):6 + 2 * (hd % 2), :]

        accp = [[ctx.enter_context(nc.psum_tensor(f"acc{a}{b}", [P, 512], F32)) for b in range(2)]
                for a in range(2)]
        side = ctx.enter_context(nc.psum_tensor("side", [P, 4, 512], F32))
        pre_junk = side[:, 2:4, :].rearrange("p a n -> p (a n)")

        def front_bank(b):
            return accp[b // 2][b % 2]

        def chunk_of(l, b):
            return cT[:, b * GH:(b + 1) * GH, l * P:(l + 1) * P]

        QN, KN, DECAY, T_, U_, AU = 0, 1, 4, 9, 10, 11
        A_S = (12, 13)
        R_, VNEW = 14, 15

        def a_of(n):
            return (5, 7)[n % 2]

        def qk_of(n):
            return (6, 8)[n % 2]

        def kd_of(n):
            return (3, 2)[n % 2]

        def bank(n):
            if n % 2:
                return [side[:, 0, :], side[:, 1, :]], side[:, 2, :], side[:, 3, :]
            return [accp[0][0][:], accp[0][1][:]], accp[1][0][:], accp[1][1][:]

        LAST = ([FFN1_0 + (h + 1) * FFN_STEPS - 1 for h in range(HALVES)]
                + [MIX_0 + (h + 1) * MIX_STEPS - 1 for h in range(HALVES)]
                + [MEM_0 + (h + 1) * MEM_STEPS - 1 for h in range(HALVES)]
                + [FFN2_0 + (h + 1) * FFN_STEPS - 1 for h in range(HALVES)])
        PRE_GAIN = (0, 0, 1, 1, 4, 2, 2, 3, 3)

        const_in = sem("const_in")
        x_in = [sem("x_in0"), sem("x_in1")]
        mem_in = sem("mem_in")
        grow_in = sem("grow_in")
        mask_st = sem("mask_st")
        neg_rdy = sem("neg_rdy")
        w_landed = [sem("w_landed0"), sem("w_landed1")]
        w_hi_ok = sem("w_hi_ok")
        w_lo_ok = sem("w_lo_ok")
        w_used = sem("w_used")
        act_evac = sem("act_evac")
        acc_free = sem("acc_free")
        act_hi_ok = sem("act_hi_ok")
        act_lo_ok = sem("act_lo_ok")
        dve_seq = sem("dve_seq")
        pre_ssq = sem("pre_ssq")
        pre_v = sem("pre_v")
        pre_rs = sem("pre_rs")
        pre_xn = sem("pre_xn")
        pre_tr = sem("pre_tr")
        pre_hi = sem("pre_hi")
        pre_lo = sem("pre_lo")
        post_tr = sem("post_tr")
        post_ssq = sem("post_ssq")
        post_v = sem("post_v")
        post_rs = sem("post_rs")
        post_x = sem("post_x")
        conv_ok = sem("conv_ok")
        conv_silu = sem("conv_silu")
        delta = {n: sem("d_" + n) for n in (
            "ab_psum",
            "ab_sbuf",
            "ab_exp",
            "g_ready",
            "g_sums",
            "g_spread",
            "g_exp",
            "beta_decay",
            "tok_major",
            "squares",
            "sumsq",
            "meansq",
            "roots",
            "qk_normed",
            "beta_v",
            "decay_exp",
            "decay",
            "decay_masked",
            "kqT_psum",
            "kqT_sbuf",
            "kk_qk",
            "A_ready",
            "qk_masked",
            "T_first",
            "U_psum",
            "U_sbuf",
            "A_block",
            "AU_psum",
            "AU_sbuf",
            "UAU_psum",
            "T_psum",
            "T_level",
            "U_level",
            "kS_qS",
            "state_decayed",
            "R_ready",
            "vnew_psum",
            "vnew_sbuf",
            "out_psum",
            "state_ready",
            "out_sbuf",
            "out_squares",
            "out_sumsq",
            "out_meansq",
            "out_roots",
            "out_normed",
            "outT_psum",
            "gated",
            "mix_hi",
            "mix_lo",
        )}
        attn = {n: sem("a_" + n) for n in (
            "v_psum",
            "v_sbuf",
            "distance",
            "log_count",
            "bias",
            "scores",
            "max",
            "neg_max",
            "probs",
            "pT_psum",
            "pT_sbuf",
            "out_psum",
            "out_sbuf",
            "outT_psum",
            "out_hi",
            "out_lo",
        )}
        memo = {n: sem("m_" + n) for n in (
            "v_psum",
            "v_sbuf",
            "scores",
            "neg_max",
            "probs",
            "probs_normed",
            "pT_psum",
            "pT_sbuf",
            "out_psum",
            "out_hi",
            "out_lo",
        )}
        out_ok = sem("out_ok")

        def wcols(w, c0, nk=KT, r0=0):
            return w[0][r0:r0 + nk * P, c0].rearrange("(k p) n -> p k n", p=P)

        def pairs_of(buf, s, second):
            return buf.rearrange("p (g t) -> p g t", t=2 * s)[:, :, s * second:s * second + s]

        def bc_h(v):
            return v.unsqueeze(2).to_broadcast([P, GH, P])

        def bc_m(m):
            return m.unsqueeze(1).to_broadcast([P, GH, P])

        def steps(eng, first, n, body):
            pairs = n // 2
            peeled = pairs if pairs < 2 else int(first == 0)
            for k in range(2 * peeled):
                body(first + k, k, (first + k) % 2)
            if peeled < pairs:
                with eng.Fori(peeled, pairs) as i:
                    body(i * 2 + first, i * 2, first % 2)
                    body(i * 2 + (first + 1), i * 2 + 1, (first + 1) % 2)
            if n % 2:
                body(first + n - 1, n - 1, (first + n - 1) % 2)

        SK = (len(CHUNKS) - 1) * (KT // 2)

        def ffn_skip(base_skip, h, c):
            return base_skip + h * SK + max(0, c - 1) * (KT // 2)

        FFN1_SKIP, MID_SKIP = 0, HALVES * SK
        FFN2_SKIP = MID_SKIP
        FSTEP = [sum(CHUNKS[:c]) + c * (KT // 2) for c in range(len(CHUNKS))]

        block = ctx.enter_context(nc.Block())

        @block.sync
        def _(sp):
            def load(p, par, blocks):
                if not isinstance(p, int) or p >= 2:
                    sp.wait_ge(w_lo_ok, p - 1)
                for dst, src in blocks:
                    sp.dma_start(dst, src).then_inc(w_landed[par], 16)

            def pair(par, nk, a, b):
                return [(w_raw[:, par, 0, 0:nk, :], a), (w_raw[:, par, 1, 0:nk, :], b)]

            def cols(j, k, base=0):
                if isinstance(j, int):
                    return slice(base + (2 * j + k) * P, base + (2 * j + k + 1) * P)
                return bass.ds(j * (2 * P) + (base + k * P), P)

            def ffn(p0, wg, wu, wd, before=None):
                f0 = 0
                for c, nf in enumerate(CHUNKS):
                    def up(p, j, par, f0=f0):
                        cs = slice((f0 + j) * P, (f0 + j + 1) * P) if isinstance(j, int) else bass.ds(j * P + f0 * P, P)
                        load(p, par, pair(par, KT, wcols(wg, cs), wcols(wu, cs)))

                    def down(p, j, par, f0=f0, nf=nf):
                        load(p, par, pair(par, nf, wcols(wd, cols(j, 0), nf, f0 * P),
                                          wcols(wd, cols(j, 1), nf, f0 * P)))
                    if p0 == 0 and c == 0:
                        for k in range(TT):
                            sp.dma_start(x[:, k, :], t["x"][0][k * P:(k + 1) * P, :]).then_inc(x_in[0], 16)
                        up(0, 0, 0)
                        up(1, 1, 1)
                        for k in range(TT, S // P):
                            sp.dma_start(x[:, k, :], t["x"][0][k * P:(k + 1) * P, :]).then_inc(x_in[1], 16)
                        steps(sp, 2, nf - 2, lambda p, j, par: up(p, j + 2, par))
                    else:
                        steps(sp, p0 + FSTEP[c], nf, up)
                    steps(sp, p0 + FSTEP[c] + nf, KT // 2, down)
                    f0 += nf

            def plain(p0, n, w, base=0):
                steps(sp, p0, n, lambda p, j, par: load(p, par, pair(
                    par, KT, wcols(w, cols(j, 0, base)), wcols(w, cols(j, 1, base)))))

            for h in range(HALVES):
                ffn(FFN1_0 + h * FFN_STEPS, t["ffn1_w_gate"], t["ffn1_w_up"], t["ffn1_w_down"])

            for h in range(HALVES):
                p0 = MIX_0 + h * MIX_STEPS
                plain(p0, GDN_STEPS, t["w_in"])
                p = p0 + GDN_STEPS
                ab = wcols(t["w_in"], slice(AB0, AB0 + 2 * GH))
                load(p, p % 2, [(w_raw[:, p % 2, 0, 0:4, 0:2 * GH], ab[:, 0:4, :]),
                                (w_raw[:, p % 2, 0, 4:8, 0:2 * GH], ab[:, 4:8, :])])
                plain(p0 + GDN_STEPS + 1, ATT_STEPS, t["w_in"], QB0)
                plain(p0 + GDN_STEPS + 1 + ATT_STEPS, KT // 2, t["w_out"])

            plain(KV_0, KT // 2, t["mem_wk"])
            plain(KV_0 + KT // 2, KT // 2, t["mem_wv"])
            for h in range(HALVES):
                plain(MEM_0 + h * MEM_STEPS, KT // 2, t["mem_wq"])
                plain(MEM_0 + h * MEM_STEPS + KT // 2, KT // 2, t["mem_wo"])

            for h in range(HALVES):
                ffn(FFN2_0 + h * FFN_STEPS, t["ffn2_w_gate"], t["ffn2_w_up"], t["ffn2_w_down"])

            for tt in range(S // P):
                sp.wait_ge(post_x, 6 * TT + tt + 1)
                sp.dma_start(t["out"][0][tt * P:(tt + 1) * P, :], x[:, tt, :]).then_inc(out_ok, 16)
            sp.wait_ge(out_ok, 16 * S // P)

        @block.gpsimd
        def _(pool):
            n_mask = [0]

            def keep(ins):
                n_mask[0] += 1
                ins.then_inc(mask_st, 1)
                pool.wait_ge(mask_st, n_mask[0])

            keep(pool.memset(half_pow[:], -0.5))
            keep(pool.memset(ones[:], 1.0))
            keep(pool.memset(ident[:], 0.0))
            keep(pool.affine_select(out=ident[:], in_=ident[:], compare_op=ALU.not_equal, fill=1.0,
                                    base=0, pattern=[[-1, P]], channel_multiplier=1))
            def level_masks():
                keep(pool.memset(carry[:], 0.0))
                keep(pool.memset(state[:], 0.0))
                keep(pool.affine_select(out=tri_u[:], in_=ones[:], compare_op=ALU.is_ge, fill=0.0,
                                        base=0, pattern=[[1, P]], channel_multiplier=-1))
                keep(pool.affine_select(out=tri_s[:], in_=ones[:], compare_op=ALU.is_gt, fill=0.0,
                                        base=0, pattern=[[-1, P]], channel_multiplier=1))
                for n, s in enumerate((1,) + LEVELS):
                    v = m_lvl[:, n, :].rearrange("p (a t) -> p a t", t=2 * s)
                    na = P // (2 * s)
                    keep(pool.affine_select(out=v, in_=ones[:].rearrange("p (a t) -> p a t", t=2 * s),
                                            compare_op=ALU.is_ge, fill=0.0, base=-s,
                                            pattern=[[-2 * s, na], [0, 2 * s]], channel_multiplier=1))
                    keep(pool.affine_select(out=v, in_=v, compare_op=ALU.is_ge, fill=0.0, base=2 * s - 1,
                                            pattern=[[2 * s, na], [0, 2 * s]], channel_multiplier=-1))
                    keep(pool.affine_select(out=v, in_=v, compare_op=ALU.is_ge, fill=0.0, base=s - 1,
                                            pattern=[[0, na], [-1, 2 * s]], channel_multiplier=0))
                assert n_mask[0] == N_CONST

            def roots(ssq, rs, n0, n, own, own_n, done, scale=1.0 / D, eps=EPS):
                pool.tensor_scalar(rs[:, n0:n0 + n], ssq[:, n0:n0 + n], scale, eps, ALU.mult, ALU.add).then_inc(own, 1)
                pool.wait_ge(own, own_n)
                pool.tensor_tensor(rs[:, n0:n0 + n], rs[:, n0:n0 + n], half_pow[:, 0:n], ALU.pow).then_inc(done, 1)

            def pre(q):
                pool.wait_ge(pre_ssq, PRE_BASE[q] + PRE_TILES[q])
                roots(ssq_pre, rs_pre, PRE_BASE[q], PRE_TILES[q], pre_v, q + 1, pre_rs)

            def post(r):
                g_row = post_bufs(r)[0]
                if r in (0, 4, 5, 6):
                    pool.wait_ge(pre_tr, {0: 2, 4: 7, 5: 8, 6: 9}[r] * KT)
                elif r == 2:
                    pool.wait_ge(w_used, MIX_0 + MIX_STEPS - 3)
                elif r == 7:
                    pool.wait_ge(post_x, 7 * TT)
                name = ("ffn1_post_g", "mix_post_g", "mem_post_g", "ffn2_post_g")[r // 2]
                pool.dma_start(g_row, t[name][0].partition_broadcast(P)).then_inc(grow_in, 16)
                for k in range(TT):
                    n = r * TT + k
                    pool.wait_ge(post_ssq, n + 1)
                    roots(ssq_post, rs_post, n, 1, post_v, n + 1, post_rs)

            def gdn(h):
                def front(l, stage):
                    n = h * TT + l
                    E, Eb, Eu, kn, kd = (arena[:, i, :].rearrange("p (h c) -> p h c", h=GH)
                                         for i in (DECAY, a_of(n), qk_of(n), KN, kd_of(n)))
                    if stage == 1:
                        pool.wait_ge(delta["sumsq"], 2 * n + 2)
                        pool.tensor_scalar(sm[:, 12, 0:4], sm[:, 10, 0:4], float(GD), EPS * GD, ALU.mult, ALU.add).then_inc(delta["meansq"], 1)
                        pool.tensor_scalar(sm[:, 12, 4:8], sm[:, 10, 4:8], 1.0, EPS, ALU.mult, ALU.add).then_inc(delta["meansq"], 1)
                        pool.wait_ge(delta["meansq"], 2 * n + 2)
                        pool.tensor_tensor(sm[:, 13, 0:8], sm[:, 12, 0:8], half_pow[:, 0:8], ALU.pow).then_inc(delta["roots"], 1)
                    elif stage == 3:
                        pool.wait_ge(delta["decay"], n + 1)
                        pool.tensor_tensor(Eb, E, bc_m(tri_s[:]), ALU.mult).then_inc(delta["decay_masked"], 1)
                        pool.tensor_tensor(Eu, E, bc_m(tri_u[:]), ALU.mult).then_inc(delta["decay_masked"], 1)
                        pool.wait_ge(delta["decay_masked"], 4 * n + 1)
                        pool.tensor_tensor(Eb, Eb, bc_h(sm[:, 1, l * 4:l * 4 + 4]), ALU.mult).then_inc(delta["decay_masked"], 1)
                    elif stage == 4:
                        pool.wait_ge(delta["qk_normed"], 2 * n + 2)
                        pool.tensor_tensor(kd, kn, bc_h(sm[:, 6, l * 4:l * 4 + 4]), ALU.mult).then_inc(delta["decay_masked"], 1)

                def output_roots(l):
                    n = h * TT + l
                    pool.wait_ge(delta["out_sumsq"], n + 1)
                    pool.tensor_scalar(sm[:, 14, 0:4], sm[:, 14, 4:8], 1.0 / GD, EPS, ALU.mult, ALU.add).then_inc(delta["out_meansq"], 1)
                    pool.wait_ge(delta["out_meansq"], n + 1)
                    pool.tensor_tensor(sm[:, 14, 8:12], sm[:, 14, 0:4], half_pow[:, 0:4], ALU.pow).then_inc(delta["out_roots"], 1)

                for stage in range(len(LEVELS)):
                    front(0, stage)
                for l in range(TT):
                    n = h * TT + l

                    def block_of_a(v):
                        pool.tensor_tensor(arena[:, A_S[v % 2], :].rearrange("p (h c) -> p h c", h=GH),
                                           arena[:, a_of(n), :].rearrange("p (h c) -> p h c", h=GH),
                                           bc_m(m_lvl[:, v + 1, :]), ALU.mult).then_inc(delta["A_block"], 1)

                    pool.wait_ge(delta["A_ready"], n + 1)
                    block_of_a(0)
                    block_of_a(1)
                    for v in range(len(LEVELS)):
                        if v + 2 < len(LEVELS):
                            pool.wait_ge(delta["AU_psum"], 6 * n + v + 1)
                            block_of_a(v + 2)
                        if l and v == 0:
                            output_roots(l - 1)
                        if l + 1 < TT:
                            front(l + 1, v)
                    pool.wait_ge(delta["kS_qS"], n + 1)
                    pool.tensor_tensor(state[:], state[:], bc_h(sm[:, 5, l * 4:l * 4 + 4]), ALU.mult).then_inc(delta["state_decayed"], 1)
                output_roots(TT - 1)

            def att(h):
                pool.wait_ge(delta["gated"], (h + 1) * TT)
                pool.iota(arena[:, 0:2, :].rearrange("p a n -> p (a n)").bitcast(I32), pattern=[[-1, S]],
                          base=S - P, channel_multiplier=1).then_inc(attn["distance"], 1)
                for hd in range(AH):
                    n = h * AH + hd
                    bias = arena[:, 2 * (hd % 2):2 * (hd % 2) + 2, :].rearrange("p a n -> p (a n)")
                    if hd >= 2:
                        pool.wait_ge(attn["max"], 4 * (n - 1))
                    else:
                        pool.wait_ge(attn["log_count"], h + 1)
                    pool.iota(bias, pattern=[[1, S]], base=P - S, channel_multiplier=-1,
                              allow_small_or_imprecise_dtypes=True).then_inc(attn["bias"], 1)
                    pool.wait_ge(attn["bias"], 3 * n + 1)
                    pool.tensor_scalar(bias, bias, 8.0 * 2.0 ** -(hd + 1), 0.0, ALU.mult, ALU.add).then_inc(attn["bias"], 1)
                    pool.wait_ge(attn["bias"], 3 * n + 2)
                    pool.wait_ge(attn["log_count"], h + 1)
                    pool.tensor_tensor(bias, bias, arena[:, 12:14, :].rearrange("p a n -> p (a n)"), ALU.add).then_inc(attn["bias"], 1)

            pre(0)
            level_masks()
            pre(1)
            post(0)
            pre(2)
            post(1)
            gdn(0)
            att(0)
            pre(3)
            post(2)
            gdn(1)
            att(1)
            pool.wait_ge(attn["out_lo"], 4 * HALVES)
            pool.dma_start(memx[:], t["mem"][0].rearrange("(t p) d -> p t d", p=P)).then_inc(mem_in, 16)
            pre(4)
            post(3)
            pre(5)
            pre(6)
            post(4)
            pre(7)
            post(5)
            pre(8)
            post(6)
            post(7)

        @block.tensor
        def _(pe):
            def mm3(out, hi, lo, xh, xl, nk):
                for k in range(nk):
                    pe.matmul(out, hi[:, k, :], xh[:, k, :], start=(k == 0), stop=False)
                    pe.matmul(out, hi[:, k, :], xl[:, k, :], start=False, stop=False)
                    last = pe.matmul(out, lo[:, k, :], xh[:, k, :], start=False, stop=(k == nk - 1))
                return last

            def step(p, par, xh, xl, nk, n=TOK, blocks=2):
                pe.wait_ge(w_lo_ok, p + 1)
                if not isinstance(p, int) or p >= 2:
                    pe.wait_ge(acc_free, p - 1)
                for b in range(blocks):
                    last = mm3(accp[par][b][:, 0:n], w_hi[:, par, b], w_lo[:, par, b], xh, xl, nk)
                last.then_inc(w_used, 1)

            def pre_k(q, k):
                if k == 0:
                    pe.wait_ge(pre_xn, PRE_BASE[q] + PRE_TILES[q])
                    if POSTS_BEFORE[q]:
                        pe.wait_ge(post_x, POSTS_BEFORE[q] * TT)
                elif k >= 4:
                    pe.wait_ge(pre_lo, q * KT + k - 3)
                for tt in range(PRE_TILES[q]):
                    last = pe.transpose(side[:, k % 4, tt * P:(tt + 1) * P], xn[:, tt, k * P:(k + 1) * P], ident[:])
                last.then_inc(pre_tr, 1)

            def pre(q):
                for k in range(KT):
                    pre_k(q, k)

            def operand(q):
                pe.wait_ge(pre_lo, (q + 1) * KT)

            def post_tile(r, k):
                if k == 0:
                    pe.wait_ge(acc_free, LAST[r] + 1)
                elif k >= 2:
                    pe.wait_ge(post_x, r * TT + k - 1)
                for d in range(KT):
                    last = pe.transpose(side[:, 2 * (k % 2) + d // 4, (d % 4) * P:(d % 4 + 1) * P],
                                        oT[:, d, k * P:(k + 1) * P], ident[:])
                last.then_inc(post_tr, 1)

            def first_down(p, nf, u0):
                par = p % 2
                pe.wait_ge(w_lo_ok, p + 1)
                pe.wait_ge(acc_free, p - 1)
                for ks in (range(nf - 1), (nf - 1,)):
                    pe.wait_ge(act_lo_ok, u0 - nf + ks[-1] + 1)
                    for b in range(2):
                        for k in ks:
                            o, hi, lo = accp[par][b][:], w_hi[:, par, b, k, :], w_lo[:, par, b, k, :]
                            pe.matmul(o, hi, act_hi[:, k, :], start=(k == 0), stop=False)
                            pe.matmul(o, hi, act_lo[:, k, :], start=False, stop=False)
                            last = pe.matmul(o, lo, act_hi[:, k, :], start=False, stop=(k == nf - 1))
                last.then_inc(w_used, 1)

            def h_step(p, j, par):
                step(p, par, h_hi, h_lo, KT)

            def ffn(p0, u0, r_prev, q_next):
                for c, nf in enumerate(CHUNKS):
                    first = p0 + FSTEP[c]
                    if c == 0 and r_prev is not None:
                        for k in range(TT):
                            h_step(first + k, k, (first + k) % 2)
                            post_tile(r_prev, k)
                        steps(pe, first + TT, nf - TT, h_step)
                    else:
                        steps(pe, first, nf, h_step)
                    u0 += nf
                    first += nf
                    if c == len(CHUNKS) - 1 and q_next is not None:
                        for j in range(KT // 2):
                            pre_k(q_next, 2 * j)
                            pre_k(q_next, 2 * j + 1)
                            if j:
                                step(first + j, (first + j) % 2, act_hi, act_lo, nf)
                            else:
                                first_down(first, nf, u0)
                    else:
                        first_down(first, nf, u0)
                        steps(pe, first + 1, KT // 2 - 1, lambda p, j, par: step(p, par, act_hi, act_lo, nf))
                return u0

            def heads(buf):
                return buf.rearrange("p (h c) -> p h c", h=GH)

            def gdn(h):
                pe.wait_ge(acc_free, MIX_0 + h * MIX_STEPS + GDN_STEPS + 1)
                for l in range(TT):
                    last = pe.transpose(side[:, 0, l * 8:l * 8 + 8], arena[0:8, 15, l * P:(l + 1) * P], ident[0:8, 0:8])
                last.then_inc(delta["ab_psum"], 1)
                pe.wait_ge(delta["g_ready"], h + 1)
                pe.matmul(side[:, 1, 0:16], tri_u[:], sm[:, 0, :], start=True, stop=True)
                pe.matmul(side[:, 2, 0:16], ones[:], sm[:, 0, :], start=True, stop=True).then_inc(delta["g_sums"], 1)
                pe.wait_ge(delta["beta_decay"], h + 1)

                def to_tokens(l, b):
                    for hd in range(GH):
                        last = pe.transpose(front_bank(b)[:, hd * P:(hd + 1) * P], chunk_of(l, b)[:, hd, :], ident[:])
                    last.then_inc(delta["tok_major"], 1)

                def to_channels(n, b, src):
                    for hd in range(GH):
                        last = pe.transpose(front_bank(b)[:, hd * P:(hd + 1) * P], arena[:, src, hd * P:(hd + 1) * P], ident[:])
                    last.then_inc(delta["kqT_psum"], 1)

                def front(l, slot):
                    n = h * TT + l
                    if slot == 1:
                        if l:
                            pe.wait_ge(delta["qk_masked"], n)
                        to_tokens(l, 0)
                    elif slot == 2:
                        to_tokens(l, 1)
                    elif slot == 3:
                        to_tokens(l, 2)
                    elif slot == 4:
                        pe.wait_ge(delta["g_spread"], n + 1)
                        for hd in range(GH):
                            last = pe.matmul(front_bank(3)[:, hd * P:(hd + 1) * P], arena[:, QN, hd * P:(hd + 1) * P], tri_u[:],
                                             start=True, stop=True)
                        last.then_inc(delta["tok_major"], 1)
                    elif slot == 9:
                        pe.wait_ge(delta["qk_normed"], 2 * n + 2)
                        to_channels(n, 0, KN)
                    elif slot == 10:
                        to_channels(n, 1, QN)
                    elif slot == 11:
                        pe.wait_ge(delta["kqT_sbuf"], 2 * n + 2)
                        pe.wait_ge(delta["beta_v"], n + 1)
                        pe.wait_ge(delta["decay_exp"], n + 1)
                        kT, qT = chunk_of(l, 1), chunk_of(l, 0)
                        for hd in range(GH):
                            hs = slice(hd * P, (hd + 1) * P)
                            pe.matmul(front_bank(2)[:, hs], kT[:, hd, :], kT[:, hd, :], start=True, stop=True)
                            last = pe.matmul(front_bank(3)[:, hs], kT[:, hd, :], qT[:, hd, :], start=True, stop=True)
                        last.then_inc(delta["kk_qk"], 1)

                def output_tr(l):
                    n = h * TT + l
                    pe.wait_ge(delta["out_normed"], n + 1)
                    for hd in range(GH):
                        last = pe.transpose(side[:, 3, hd * P:(hd + 1) * P], chunk_of(l, 2)[:, hd, :], ident[:])
                    last.then_inc(delta["outT_psum"], 1)

                pe.wait_ge(acc_free, MIX_0 + h * MIX_STEPS + GDN_STEPS + 1)
                for slot in range(2 * len(LEVELS)):
                    front(0, slot)
                for l in range(TT):
                    n = h * TT + l
                    if l:
                        pe.wait_ge(delta["out_sbuf"], n)
                    pe.wait_ge(delta["T_first"], n + 1)
                    for hd in range(GH):
                        hs = slice(hd * P, (hd + 1) * P)
                        last = pe.transpose(side[:, 0, hs], arena[:, T_, hs], ident[:])
                    last.then_inc(delta["U_psum"], 1)
                    pe.wait_ge(delta["U_sbuf"], n + 1)
                    for v, s in enumerate(LEVELS):
                        m = 6 * n + v
                        pe.wait_ge(delta["A_block"], m + 1)
                        if v:
                            pe.wait_ge(delta["U_level"], m)
                        for hd in range(GH):
                            hs = slice(hd * P, (hd + 1) * P)
                            last = pe.matmul(pairs_of(side[:, 0, hs], s, 1), arena[:, A_S[v % 2], hs],
                                             pairs_of(arena[:, U_, hs], s, 1), start=True, stop=True)
                        last.then_inc(delta["AU_psum"], 1)
                        if v:
                            for hd in range(GH):
                                hs = slice(hd * P, (hd + 1) * P)
                                last = pe.transpose(side[:, 2, hs], arena[:, U_, hs], ident[:])
                            last.then_inc(delta["T_psum"], 1)
                        if l + 1 < TT:
                            front(l + 1, 2 * v)
                        if l and v == 3:
                            output_tr(l - 1)
                        if v:
                            pe.wait_ge(delta["T_level"], 5 * n + v)
                        pe.wait_ge(delta["AU_sbuf"], m + 1)
                        for hd in range(GH):
                            hs = slice(hd * P, (hd + 1) * P)
                            last = pe.matmul(pairs_of(side[:, 1, hs], s, 1), arena[:, T_, hs],
                                             pairs_of(arena[:, AU, hs], s, 1), start=True, stop=True)
                        last.then_inc(delta["UAU_psum"], 1)
                        if l + 1 < TT:
                            front(l + 1, 2 * v + 1)
                    pe.wait_ge(delta["U_level"], 6 * n + 6)
                    pe.wait_ge(delta["qk_masked"], n + 1)
                    if n:
                        pe.wait_ge(delta["state_ready"], n)
                    if l:
                        pe.wait_ge(delta["gated"], n)
                    for hd in range(GH):
                        hs = slice(hd * P, (hd + 1) * P)
                        pe.matmul(side[:, 0, hs], chunk_of(l, 1)[:, hd, :], state[:, hd, :], start=True, stop=True)
                        last = pe.matmul(side[:, 3, hs], chunk_of(l, 0)[:, hd, :], state[:, hd, :], start=True, stop=True)
                    last.then_inc(delta["kS_qS"], 1)
                    pe.wait_ge(delta["R_ready"], n + 1)
                    for hd in range(GH):
                        hs = slice(hd * P, (hd + 1) * P)
                        last = pe.matmul(side[:, 1, hs], arena[:, U_, hs], arena[:, R_, hs], start=True, stop=True)
                    last.then_inc(delta["vnew_psum"], 1)
                    pe.wait_ge(delta["vnew_sbuf"], n + 1)
                    pe.wait_ge(delta["decay_masked"], 4 * n + 4)
                    for hd in range(GH):
                        hs = slice(hd * P, (hd + 1) * P)
                        pe.matmul(side[:, 0, hs], arena[:, kd_of(n), hs], arena[:, VNEW, hs], start=True, stop=True)
                        last = pe.matmul(side[:, 2, hs], arena[:, qk_of(n), hs], arena[:, VNEW, hs], start=True, stop=True)
                    last.then_inc(delta["out_psum"], 1)
                output_tr(TT - 1)

            def att(h):
                units = [(hd, i) for hd in range(AH) for i in range(TT)]

                def qk(u):
                    hd, i = units[u]
                    n = h * len(units) + u
                    nk = h * TT + i + 1
                    rows = slice(64 * (hd % 2), 64 * (hd % 2) + 64)
                    sc, _, _ = bank(n)
                    if u >= 2:
                        pe.wait_ge(attn["max"], n - 1)
                    for hh in range(h + 1):
                        m = min(nk - hh * TT, TT) * P
                        last = pe.matmul(sc[hh][:, 0:m], qbT[rows, hd // 2, i * P:(i + 1) * P],
                                         kb[hh][rows, hd // 2, 0:m], start=True, stop=True)
                    last.then_inc(attn["scores"], 1)

                def key_tiles(u, g):
                    return range(g * TT, min(h * TT + u % TT + 1, (g + 1) * TT))

                def p_transposed(u, g):
                    n = h * len(units) + u
                    pbuf = arena[:, 4 + 2 * (n % 2):6 + 2 * (n % 2), :].rearrange("p a (c q) -> p (a c) q", q=P)
                    for c in key_tiles(u, g):
                        last = pe.transpose(bank(n)[1][:, (c % TT) * P:(c % TT + 1) * P], pbuf[:, c, :], ident[:])
                    last.then_inc(attn["pT_psum"], 1)

                def pv(u, g):
                    hd, i = units[u]
                    n = h * len(units) + u
                    tbuf = arena[:, 8 + 2 * (n % 2):10 + 2 * (n % 2), :].rearrange("p a (c q) -> p (a c) q", q=P)
                    if g == 0 and u >= 2:
                        pe.wait_ge(attn["out_sbuf"], n - 1)
                    pe.wait_ge(attn["pT_sbuf"], PT_N[h] + (h + 1) * u + g + 1)
                    for c in key_tiles(u, g):
                        last = pe.matmul(bank(n)[2][:, 0:AD], tbuf[:, c, :], vn[c // TT][:, c % TT, hd * AD:(hd + 1) * AD],
                                         start=(c == 0), stop=(c == h * TT + i))
                    if g == h:
                        last.then_inc(attn["out_psum"], 1)

                pe.wait_ge(delta["gated"], (h + 1) * TT)
                qk(0)
                qk(1)
                for l in range(TT):
                    if l >= 2:
                        pe.wait_ge(attn["v_sbuf"], h * TT + l - 1)
                    for b in range(4):
                        last = pe.transpose(side[:, 2 + l % 2, b * P:(b + 1) * P], arena[:, 8 + b, l * P:(l + 1) * P], ident[:])
                    last.then_inc(attn["v_psum"], 1)
                pe.wait_ge(attn["v_sbuf"], (h + 1) * TT)
                for u in range(len(units)):
                    pe.wait_ge(attn["probs"], h * len(units) + u + 1)
                    if u >= 2:
                        pe.wait_ge(attn["pT_sbuf"], PT_N[h] + (h + 1) * (u - 1))
                    p_transposed(u, 0)
                    if u:
                        pv(u - 1, h)
                    if u + 2 < len(units):
                        qk(u + 2)
                    if h:
                        pe.wait_ge(attn["pT_sbuf"], PT_N[h] + (h + 1) * u + 1)
                        p_transposed(u, 1)
                        pv(u, 0)
                pv(len(units) - 1, h)
                pe.wait_ge(attn["out_sbuf"], (h + 1) * len(units))
                for b in range(4):
                    if b >= 2:
                        pe.wait_ge(attn["out_lo"], h * 4 + b - 1)
                    for i in range(TT):
                        last = pe.transpose(side[:, b % 2, i * P:(i + 1) * P], onat[:, i, b * P:(b + 1) * P], ident[:])
                    last.then_inc(attn["outT_psum"], 1)
                pe.wait_ge(attn["out_lo"], (h + 1) * 4)
                pe.wait_ge(delta["mix_lo"], (h + 1))

            def mem(h):
                units = [(hd, i) for hd in range(MH) for i in range(TT)]

                def qk(u):
                    hd, i = units[u]
                    n = h * len(units) + u
                    if u >= 2:
                        pe.wait_ge(memo["probs"], n - 1)
                    for k in range(2):
                        last = pe.matmul(side[:, u % 2, 0:NMEM], qmT[:, 2 * hd + k, i * P:(i + 1) * P], kmT[:, 2 * hd + k, :],
                                         start=(k == 0), stop=(k == 1))
                    last.then_inc(memo["scores"], 1)

                pe.wait_ge(acc_free, MEM_0 + h * MEM_STEPS + KT // 2)
                qk(0)
                qk(1)
                for u, (hd, i) in enumerate(units):
                    n = h * len(units) + u
                    pe.wait_ge(memo["probs_normed"], n + 1)
                    if u >= 2:
                        pe.wait_ge(memo["pT_sbuf"], n - 1)
                    for c in range(2):
                        last = pe.transpose(side[:, 2 + u % 2, c * P:(c + 1) * P], arena[:, u % 2, c * P:(c + 1) * P], ident[:])
                    last.then_inc(memo["pT_psum"], 1)
                    if u + 2 < len(units):
                        qk(u + 2)
                    if i == TT - 1:
                        pe.wait_ge(memo["pT_sbuf"], n + 1)
                        for d in range(2):
                            o = h * 8 + 2 * hd + d
                            if o % 8 >= 2:
                                pe.wait_ge(memo["out_lo"], o - 1)
                            for c in range(2):
                                last = pe.matmul(accp[d][0][:], vm[:, c, hd * MD + d * P:hd * MD + (d + 1) * P],
                                                 ptm(hd)[:, c, :], start=(c == 0), stop=(c == 1))
                            last.then_inc(memo["out_psum"], 1)
                pe.wait_ge(memo["out_lo"], (h + 1) * 8)

            pe.wait_ge(mask_st, N_IDENT)
            u0 = 0
            pre(0)
            operand(0)
            u0 = ffn(FFN1_0, u0, None, 1)
            operand(1)
            u0 = ffn(FFN1_0 + FFN_STEPS, u0, 0, 2)
            pe.wait_ge(mask_st, N_CONST)
            for h in range(HALVES):
                p0 = MIX_0 + h * MIX_STEPS
                operand(2 + h)
                for k in range(TT):
                    h_step(p0 + k, k, (p0 + k) % 2)
                    post_tile(1 + h, k)
                steps(pe, p0 + TT, GDN_STEPS - TT, h_step)
                p = p0 + GDN_STEPS
                step(p, p % 2, h_hi, h_lo, KT, blocks=1)
                pe.wait_ge(post_x, (2 + h) * TT)
                gdn(h)
                steps(pe, p + 1, ATT_STEPS, lambda p, j, par: step(p, par, h_hi, h_lo, KT))
                pe.wait_ge(acc_free, p + 1 + ATT_STEPS)
                att(h)
                steps(pe, p + 1 + ATT_STEPS, KT // 2, h_step)
                pre(3 + h)
            operand(4)

            def kv_step(p, j, par):
                step(p, par, h_hi[:, :, 0:NMEM], h_lo[:, :, 0:NMEM], KT, NMEM)
            for k in range(TT):
                kv_step(KV_0 + k, k, (KV_0 + k) % 2)
                post_tile(3, k)
            steps(pe, KV_0 + TT, KV_STEPS - TT, kv_step)
            pe.wait_ge(post_x, 4 * TT)
            pe.wait_ge(acc_free, MEM_0)
            for c in range(2):
                for k in range(KT):
                    last = pe.transpose(side[:, 2 * c + k // 4, (k % 4) * P:(k % 4 + 1) * P], qmT[:, k, c * P:(c + 1) * P], ident[:])
                last.then_inc(memo["v_psum"], 1)
            for h in range(HALVES):
                p0 = MEM_0 + h * MEM_STEPS
                if h == 0:
                    pe.wait_ge(memo["v_sbuf"], 2)
                    pre(5)
                operand(5 + h)
                for k in range(KT // 2):
                    h_step(p0 + k, k, (p0 + k) % 2)
                    if h:
                        post_tile(4, k)
                if h:
                    pe.wait_ge(post_x, 5 * TT)
                mem(h)
                steps(pe, p0 + KT // 2, KT // 2, h_step)
                pre(6 + h)
            operand(7)
            u0 = ffn(FFN2_0, u0, 5, 8)
            operand(8)
            u0 = ffn(FFN2_0 + FFN_STEPS, u0, 6, None)
            pe.wait_ge(post_x, 7 * TT)
            for k in range(TT):
                post_tile(7, k)

        @block.scalar
        def _(act):
            def prep(p, par):
                if isinstance(p, int) and p >= STEPS:
                    return
                act.wait_ge(w_landed[par], (p // 2 + 1) * 32 if isinstance(p, int) else p * 16 + (32 - 16 * par))
                if not isinstance(p, int) or p >= 2:
                    act.wait_ge(w_used, p - 1)
                act.activation(w_hi[:, par].rearrange("p b k n -> p (b k n)"),
                               w_raw[:, par].rearrange("p b k n -> p (b k n)"), ACT.Copy).then_inc(w_hi_ok, 1)

            def copy2(out, in_, s):
                act.activation(out, in_, ACT.Copy).then_inc(s, 1)

            def pre_a(q):
                n0, nt = PRE_BASE[q], PRE_TILES[q]
                if q == 4:
                    act.wait_ge(mem_in, 16)
                if q < 2:
                    act.wait_ge(x_in[q], 16 * TT)
                if POSTS_BEFORE[q]:
                    act.wait_ge(post_x, POSTS_BEFORE[q] * TT)
                for k in range(nt):
                    src = memx[:, k, :] if q == 4 else x[:, (TT * (q % 2) if q < 4 else TT * ((q + 1) % 2)) + k, :]
                    if n0 + k:
                        act.wait_ge(pre_ssq, n0 + k)
                    act.activation(pre_junk, src, ACT.Square, accum_out=ssq_pre[:, n0 + k:n0 + k + 1]).then_inc(pre_ssq, 1)

            def pre_k(q, k):
                w = PRE_TILES[q] * P
                act.wait_ge(pre_tr, q * KT + k + 1)
                act.activation(h_hi[:, k, 0:w], side[:, k % 4, 0:w], ACT.Copy,
                               scale=g_pre[:, PRE_GAIN[q], k:k + 1]).then_inc(pre_hi, 1)

            def pre_b(q):
                for k in range(KT):
                    pre_k(q, k)

            def post_tile(r, k):
                n = r * TT + k
                act.wait_ge(post_tr, n + 1)
                if n:
                    act.wait_ge(post_ssq, n)
                act.activation(post_bufs(r)[2], side[:, 2 * (k % 2):2 * (k % 2) + 2, :].rearrange("p a n -> p (a n)"),
                               ACT.Square, accum_out=ssq_post[:, n:n + 1]).then_inc(post_ssq, 1)

            def ffn(p0, r_prev, q_next):
                for c, nf in enumerate(CHUNKS):
                    def up(p, j, par, prep_at=1):
                        if prep_at == 1:
                            prep(p + 1, 1 - par)
                        act.wait_ge(w_used, p + 1)
                        act.activation(sg[:, par, :], accp[par][0][:], ACT.Silu).then_inc(act_evac, 1)
                        act.wait_ge(acc_free, p + 1)
                        dst = act_hi[:, j, :] if isinstance(j, int) else act_hi[:, bass.ds(j, 1), :].rearrange("p a n -> p (a n)")
                        act.activation(dst, prod[:, par, :], ACT.Copy).then_inc(act_hi_ok, 1)
                        if prep_at == 2:
                            prep(p + 2, par)

                    def down(p, j, par):
                        prep(p + 1, 1 - par)
                        if c == 0:
                            act.wait_ge(w_used, p + 1)
                            dst = oT[:, 2 * j, :] if isinstance(j, int) else oT[:, bass.ds(j * 2, 1), :].rearrange("p a n -> p (a n)")
                            act.activation(dst, accp[par][0][:], ACT.Copy).then_inc(act_evac, 1)
                    first = p0 + FSTEP[c]
                    if c == 0 and r_prev is not None:
                        prep(first + 1, 1 - first % 2)
                        for k in range(TT):
                            up(first + k, k, (first + k) % 2, 2 if k < TT - 1 else 0)
                            post_tile(r_prev, k)
                        steps(act, first + TT, nf - TT, lambda p, j, par: up(p, j + TT, par))
                    else:
                        if c == len(CHUNKS) - 1 and q_next is not None:
                            pre_a(q_next)
                        steps(act, first, nf, up)
                    first += nf
                    if c == len(CHUNKS) - 1:
                        for k in range(KT // 2):
                            if q_next is not None:
                                pre_k(q_next, 2 * k)
                                pre_k(q_next, 2 * k + 1)
                            down(first + k, k, (first + k) % 2)
                    else:
                        steps(act, first, KT // 2, down)

            def plain(p0, n, dst, cols=TOK, r_prev=None, q_next=None, ahead=False, two=False):
                def body(p, j, par, prep_at=1):
                    if prep_at == 1:
                        prep(p + 1, 1 - par)
                    act.wait_ge(w_used, p + 1)
                    d = dst[:, 2 * j, 0:cols] if isinstance(j, int) else dst[:, bass.ds(j * 2, 1), 0:cols].rearrange("p a n -> p (a n)")
                    act.activation(d, accp[par][0][:, 0:cols], ACT.Copy).then_inc(act_evac, 1)
                    if prep_at == 2:
                        prep(p + 2, par)
                if two:
                    if not ahead:
                        prep(p0 + 1, 1 - p0 % 2)
                    for k in range(n):
                        body(p0 + k, k, (p0 + k) % 2, 2)
                        if r_prev is not None:
                            post_tile(r_prev, k)
                        elif k == 0:
                            pre_a(q_next)
                elif q_next is None and not ahead:
                    steps(act, p0, n, body)
                else:
                    for k in range(n):
                        if q_next is not None and k == n // 2:
                            pre_a(q_next)
                        body(p0 + k, k, (p0 + k) % 2, 0 if ahead and k == 0 else 1)

            def mix_in(h):
                p0 = MIX_0 + h * MIX_STEPS
                prep(p0 + 1, 1 - p0 % 2)
                for j in range(6):
                    p, n = p0 + j, h * 6 + j
                    par = p % 2
                    act.wait_ge(w_used, p + 1)
                    raw = rawc(par)
                    act.activation(raw[:, 0, 3:3 + TOK], accp[par][0][:], ACT.Copy)
                    act.activation(raw[:, 1, 3:3 + TOK], accp[par][1][:], ACT.Copy).then_inc(act_evac, 1)
                    prep(p + 2, par)
                    act.wait_ge(conv_ok, n + 1)
                    act.activation(cT[:, 2 * j:2 * j + 2, :], yconv, ACT.Silu).then_inc(conv_silu, 1)
                    if j < TT:
                        post_tile(1 + h, j)
                for j in range(2):
                    p = p0 + 6 + j
                    par = p % 2
                    act.wait_ge(w_used, p + 1)
                    act.activation(zT[:, 2 * j, :], accp[par][0][:], ACT.Silu)
                    act.activation(zT[:, 2 * j + 1, :], accp[par][1][:], ACT.Silu).then_inc(act_evac, 1)
                    prep(p + 2, par)
                p = p0 + GDN_STEPS
                act.wait_ge(w_used, p + 1)
                act.activation(arena[0:8, 14, :], accp[p % 2][0][0:8, :], ACT.Copy).then_inc(act_evac, 1)

            def gdn(h):
                act.wait_ge(delta["ab_psum"], h + 1)
                act.activation(sm[:, 16:18, :].rearrange("p a n -> p (a n)"), side[:, 0, 0:32], ACT.Copy).then_inc(delta["ab_sbuf"], 1)
                act.wait_ge(delta["ab_exp"], 2 * h + 1)
                act.activation(sm[:, 3, :], sm[:, 3, :], ACT.Exp)
                act.activation(sm[:, 2, :], sm[:, 2, :], ACT.Exp).then_inc(delta["ab_exp"], 1)
                act.wait_ge(delta["g_exp"], 2 * h + 1)
                act.activation(sm[:, 4, :], sm[:, 7, :], ACT.Exp)
                act.activation(sm[:, 5, :], sm[:, 8, :], ACT.Exp)
                act.activation(sm[:, 6, :], sm[:, 9, :], ACT.Exp).then_inc(delta["g_exp"], 1)
                def front(l, stage):
                    n = h * TT + l
                    if stage == 1:
                        act.wait_ge(delta["tok_major"], 4 * n + 1)
                        act.activation(arena[:, DECAY, :], front_bank(0)[:], ACT.Square).then_inc(delta["squares"], 1)
                        act.wait_ge(delta["tok_major"], 4 * n + 2)
                        act.activation(arena[:, a_of(n), :], front_bank(1)[:], ACT.Square).then_inc(delta["squares"], 1)
                    elif stage == 3:
                        act.wait_ge(delta["decay_exp"], n + 1)
                        act.activation(arena[:, DECAY, :], arena[:, qk_of(n), :], ACT.Exp).then_inc(delta["decay"], 1)
                    elif stage == 4:
                        act.wait_ge(delta["kqT_psum"], 2 * n + 1)
                        copy2(chunk_of(l, 1), front_bank(0)[:].rearrange("p (h c) -> p h c", h=GH), delta["kqT_sbuf"])
                        act.wait_ge(delta["kqT_psum"], 2 * n + 2)
                        copy2(chunk_of(l, 0), front_bank(1)[:].rearrange("p (h c) -> p h c", h=GH), delta["kqT_sbuf"])

                for stage in range(len(LEVELS)):
                    front(0, stage)
                for l in range(TT):
                    n = h * TT + l
                    act.wait_ge(delta["U_psum"], n + 1)
                    copy2(arena[:, U_, :], side[:, 0, :], delta["U_sbuf"])
                    for v, s in enumerate(LEVELS):
                        m = 6 * n + v
                        act.wait_ge(delta["AU_psum"], m + 1)
                        if v == 0 and n:
                            act.wait_ge(delta["UAU_psum"], m)
                        copy2(pairs_of(arena[:, AU, :], s, 1), pairs_of(side[:, 0, :], s, 1), delta["AU_sbuf"])
                        if l + 1 < TT:
                            front(l + 1, v)
                    act.wait_ge(delta["vnew_psum"], n + 1)
                    copy2(arena[:, VNEW, :], side[:, 1, :], delta["vnew_sbuf"])
                    act.wait_ge(delta["out_sbuf"], n + 1)
                    act.activation(chunk_of(l, 1), chunk_of(l, 0), ACT.Square).then_inc(delta["out_squares"], 1)

            def att(h):
                act.wait_ge(delta["gated"], (h + 1) * TT)
                act.activation(h_hi[:, 0:4, :], zT[:], ACT.Copy).then_inc(delta["mix_hi"], 1)
                for l in range(TT):
                    act.wait_ge(attn["v_psum"], h * TT + l + 1)
                    copy2(vn[h][:, l, :], side[:, 2 + l % 2, :], attn["v_sbuf"])
                n_units = AH * TT
                def exp(u):
                    n = h * n_units + u
                    nk = h * TT + u % TT + 1
                    pb = arena[:, 4 + 2 * (n % 2):6 + 2 * (n % 2), :].rearrange("p a n -> p (a n)")
                    act.wait_ge(attn["neg_max"], n + 1)
                    act.activation(pb[:, 0:nk * P], pb[:, 0:nk * P], ACT.Exp, bias=sm[:, 19, n % 2:n % 2 + 1], scale=AD ** -0.5,
                                   accum_out=sm[:, 20, n % 4:n % 4 + 1]).then_inc(attn["probs"], 1)

                exp(0)
                for u in range(n_units):
                    n = h * n_units + u
                    nk = h * TT + u % TT + 1
                    if u + 1 < n_units:
                        exp(u + 1)
                    tb = arena[:, 8 + 2 * (n % 2):10 + 2 * (n % 2), :]
                    _, ptb, _ = bank(n)
                    for g in range(h + 1):
                        m = min(nk - g * TT, TT) * P
                        act.wait_ge(attn["pT_psum"], PT_N[h] + (h + 1) * u + g + 1)
                        copy2(tb[:, g, 0:m], ptb[:, 0:m], attn["pT_sbuf"])
                for b in range(4):
                    act.wait_ge(attn["outT_psum"], h * 4 + b + 1)
                    act.activation(h_hi[:, 4 + b, :], side[:, b % 2, :], ACT.Copy).then_inc(attn["out_hi"], 1)

            def mem(h):
                n_units = MH * TT
                def exp(u):
                    n = h * n_units + u
                    act.wait_ge(memo["neg_max"], n + 1)
                    act.activation(arena[:, u % 2, 0:NMEM], side[:, u % 2, 0:NMEM], ACT.Exp, bias=sm[:, 19, n % 2:n % 2 + 1],
                                   scale=MD ** -0.5, accum_out=sm[:, 20, n % 2:n % 2 + 1]).then_inc(memo["probs"], 1)

                exp(0)
                for u in range(n_units):
                    n = h * n_units + u
                    hd, i = u // TT, u % TT
                    if u + 1 < n_units:
                        exp(u + 1)
                    act.wait_ge(memo["pT_psum"], n + 1)
                    act.activation(ptm(hd)[:, :, i * P:(i + 1) * P], side[:, 2 + u % 2, 0:NMEM].rearrange("p (c q) -> p c q", c=2),
                                   ACT.Copy).then_inc(memo["pT_sbuf"], 1)
                    if i == TT - 1:
                        for d in range(2):
                            o = h * 8 + 2 * hd + d
                            act.wait_ge(memo["out_psum"], o + 1)
                            act.activation(h_hi[:, 2 * hd + d, :], accp[d][0][:], ACT.Copy).then_inc(memo["out_hi"], 1)

            act.dma_start(g_pre[:, 0, :], t["ffn1_pre_g"][0].rearrange("(k p) -> p k", p=P)).then_inc(const_in, 16)
            act.dma_start(g_pre[:, 1, :], t["mix_pre_g"][0].rearrange("(k p) -> p k", p=P)).then_inc(const_in, 16)
            act.dma_start(g_pre[:, 2, :], t["mem_pre_g"][0].rearrange("(k p) -> p k", p=P)).then_inc(const_in, 16)
            act.dma_start(g_pre[:, 3, :], t["ffn2_pre_g"][0].rearrange("(k p) -> p k", p=P)).then_inc(const_in, 16)
            act.dma_start(g_pre[:, 4, :], t["mem_kv_g"][0].rearrange("(k p) -> p k", p=P)).then_inc(const_in, 16)
            for j in range(4):
                act.dma_start(conv_w[:, :, j], t["gdn_conv_w"][0][j].rearrange("(k p) -> p k", p=P)).then_inc(const_in, 16)
            act.dma_start(ngain[:], t["gdn_norm_g"][0].rearrange("(p a) -> p a", a=1)).then_inc(const_in, 16)
            act.dma_start(dt_row[:], t["gdn_dt_bias"][0].partition_broadcast(P)).then_inc(const_in, 16)
            act.dma_start(neg_a[:], t["gdn_a_log"][0].partition_broadcast(P)).then_inc(const_in, 16)
            pre_a(0)
            prep(0, 0)
            act.wait_ge(const_in, 16 * N_SMALL)
            pre_b(0)
            ffn(FFN1_0, None, 1)
            ffn(FFN1_0 + FFN_STEPS, 0, 2)
            act.activation(neg_a[:], neg_a[:], ACT.Exp).then_inc(neg_rdy, 1)
            for h in range(HALVES):
                p0 = MIX_0 + h * MIX_STEPS
                mix_in(h)
                gdn(h)
                p = p0 + GDN_STEPS + 1
                plain(p, 2, qbT)
                plain(p + 2, 2, kb[h])
                plain(p + 4, 2, arena[:, 8:12, :])
                att(h)
                plain(p + ATT_STEPS, KT // 2, oT, q_next=3 + h)
                pre_b(3 + h)
            plain(KV_0, KT // 2, kmT, NMEM, r_prev=3, two=True)
            plain(KV_0 + KT // 2, KT // 2, qmT, NMEM, q_next=5, ahead=True, two=True)
            for h in range(HALVES):
                p0 = MEM_0 + h * MEM_STEPS
                if h == 0:
                    for c in range(2):
                        act.wait_ge(memo["v_psum"], c + 1)
                        copy2(vm[:, c, :], side[:, 2 * c:2 * c + 2, :].rearrange("p a n -> p (a n)"), memo["v_sbuf"])
                    pre_b(5)
                plain(p0, KT // 2, qmT, r_prev=4 if h else None, ahead=(h == 0), two=(h == 1))
                mem(h)
                plain(p0 + KT // 2, KT // 2, oT, q_next=6 + h, ahead=(h == 1))
                pre_b(6 + h)
            ffn(FFN2_0, 5, 8)
            ffn(FFN2_0 + FFN_STEPS, 6, None)
            for k in range(TT):
                post_tile(7, k)

        @block.vector
        def _(dve):
            n_seq = [0]

            def link(ins):
                n_seq[0] += 1
                ins.then_inc(dve_seq, 1)
                dve.wait_ge(dve_seq, n_seq[0])

            def prep(p, par):
                if isinstance(p, int) and p >= STEPS:
                    return
                dve.wait_ge(w_hi_ok, p + 1)
                dve.tensor_tensor(w_lo[:, par].rearrange("p b k n -> p (b k n)"),
                                  w_raw[:, par].rearrange("p b k n -> p (b k n)"),
                                  w_hi[:, par].bitcast(F32).rearrange("p b k n -> p (b k n)"),
                                  ALU.subtract).then_inc(w_lo_ok, 1)

            def lo_of(out, src, hi, s):
                dve.tensor_tensor(out, src, hi.bitcast(F32), ALU.subtract).then_inc(s, 1)

            def pre_a(q):
                n0, nt = PRE_BASE[q], PRE_TILES[q]
                if POSTS_BEFORE[q]:
                    dve.wait_ge(post_x, POSTS_BEFORE[q] * TT)
                dve.wait_ge(pre_rs, q + 1)
                for k in range(nt):
                    src = memx[:, k, :] if q == 4 else x[:, (TT * (q % 2) if q < 4 else TT * ((q + 1) % 2)) + k, :]
                    dve.tensor_scalar(xn[:, k, :], src, rs_pre[:, n0 + k:n0 + k + 1], None, ALU.mult).then_inc(pre_xn, 1)
            def pre_k(q, k):
                w = PRE_TILES[q] * P
                dve.wait_ge(pre_hi, q * KT + k + 1)
                dve.scalar_tensor_tensor(out=h_lo[:, k, 0:w], in0=side[:, k % 4, 0:w], scalar=g_pre[:, PRE_GAIN[q], k:k + 1],
                                         in1=h_hi[:, k, 0:w].bitcast(F32), op0=ALU.mult, op1=ALU.subtract).then_inc(pre_lo, 1)

            def pre_b(q):
                for k in range(KT):
                    pre_k(q, k)

            def post_tile(r, k):
                g_row, post_tmp, _ = post_bufs(r)
                dve.wait_ge(grow_in, 16 * (r + 1))
                n = r * TT + k
                xt = x[:, (r % 2) * TT + k, :]
                dve.wait_ge(post_rs, n + 1)
                if n:
                    dve.wait_ge(post_x, n)
                link(dve.scalar_tensor_tensor(out=post_tmp, in0=side[:, 2 * (k % 2):2 * (k % 2) + 2, :].rearrange("p a n -> p (a n)"),
                                              scalar=rs_post[:, n:n + 1], in1=g_row, op0=ALU.mult, op1=ALU.mult))
                dve.scalar_tensor_tensor(out=xt, in0=post_tmp, scalar=0.5 if r // 2 in (0, 3) else 1.0, in1=xt,
                                         op0=ALU.mult, op1=ALU.add).then_inc(post_x, 1)

            def ffn(p0, skip, h, u0, r_prev, q_next):
                for c, nf in enumerate(CHUNKS):
                    sk = ffn_skip(skip, h, c)

                    def up(p, j, par, prep_at=1):
                        if prep_at == 1:
                            prep(p + 1, 1 - par)
                        dve.wait_ge(act_evac, p + (1 - sk))
                        dve.tensor_tensor(prod[:, par, :], accp[par][1][:], sg[:, par, :], ALU.mult).then_inc(acc_free, 1)
                        dve.wait_ge(act_hi_ok, j + (u0 + 1))
                        dst = act_lo[:, j, :] if isinstance(j, int) else act_lo[:, bass.ds(j, 1), :].rearrange("p a n -> p (a n)")
                        hi = act_hi[:, j, :] if isinstance(j, int) else act_hi[:, bass.ds(j, 1), :].rearrange("p a n -> p (a n)")
                        dve.tensor_tensor(dst, prod[:, par, :], hi.bitcast(F32), ALU.subtract).then_inc(act_lo_ok, 1)
                        if prep_at == 2:
                            prep(p + 2, par)

                    def down(p, j, par):
                        prep(p + 1, 1 - par)
                        dve.wait_ge(w_used, p + 1)

                        def ot(k):
                            return oT[:, 2 * j + k, :] if isinstance(j, int) else oT[:, bass.ds(j * 2 + k, 1), :].rearrange("p a n -> p (a n)")
                        if c == 0:
                            dve.wait_ge(act_evac, p + (1 - sk))
                            dve.tensor_copy(ot(1), accp[par][1][:]).then_inc(acc_free, 1)
                        else:
                            dve.tensor_tensor(ot(0), accp[par][0][:], ot(0), ALU.add)
                            dve.tensor_tensor(ot(1), accp[par][1][:], ot(1), ALU.add).then_inc(acc_free, 1)
                    first = p0 + FSTEP[c]
                    if c == 0 and r_prev is not None:
                        prep(first + 1, 1 - first % 2)
                        for k in range(TT):
                            up(first + k, k, (first + k) % 2, 2 if k < TT - 1 else 0)
                            post_tile(r_prev, k)
                        steps(dve, first + TT, nf - TT, lambda p, j, par: up(p, j + TT, par))
                    else:
                        if c == len(CHUNKS) - 1 and q_next is not None:
                            pre_a(q_next)
                        steps(dve, first, nf, up)
                    u0 += nf
                    first += nf
                    if c == len(CHUNKS) - 1:
                        for k in range(KT // 2):
                            if q_next is not None:
                                pre_k(q_next, 2 * k)
                                pre_k(q_next, 2 * k + 1)
                            down(first + k, k, (first + k) % 2)
                    else:
                        steps(dve, first, KT // 2, down)
                return u0

            def plain(p0, n, dst, cols=TOK, r_prev=None, q_next=None, ahead=False, two=False):
                def body(p, j, par, prep_at=1):
                    if prep_at == 1:
                        prep(p + 1, 1 - par)
                    dve.wait_ge(act_evac, p + (1 - MID_SKIP))
                    d = dst[:, 2 * j + 1, 0:cols] if isinstance(j, int) else dst[:, bass.ds(j * 2 + 1, 1), 0:cols].rearrange("p a n -> p (a n)")
                    dve.tensor_copy(d, accp[par][1][:, 0:cols]).then_inc(acc_free, 1)
                    if prep_at == 2:
                        prep(p + 2, par)
                if two:
                    if not ahead:
                        prep(p0 + 1, 1 - p0 % 2)
                    for k in range(n):
                        body(p0 + k, k, (p0 + k) % 2, 2)
                        if r_prev is not None:
                            post_tile(r_prev, k)
                        elif k == 0:
                            pre_a(q_next)
                elif q_next is None and not ahead:
                    steps(dve, p0, n, body)
                else:
                    for k in range(n):
                        if q_next is not None and k == n // 2:
                            pre_a(q_next)
                        body(p0 + k, k, (p0 + k) % 2, 0 if ahead and k == 0 else 1)

            def mix_in(h):
                p0 = MIX_0 + h * MIX_STEPS
                prep(p0 + 1, 1 - p0 % 2)
                for j in range(6):
                    p, n = p0 + j, h * 6 + j
                    par = p % 2
                    raw = rawc(par)
                    ct = slice(2 * j, 2 * j + 2)
                    if n:
                        dve.wait_ge(conv_ok, n)
                    link(dve.tensor_copy(raw[:, :, 0:3], carry[:, ct, :]))
                    dve.wait_ge(act_evac, p + 1 - MID_SKIP)
                    dve.tensor_copy(carry[:, ct, :], raw[:, :, TOK:TOK + 3]).then_inc(acc_free, 1)
                    dve.wait_ge(acc_free, p + 1)
                    if n:
                        dve.wait_ge(conv_silu, n)
                    for tap in range(4):
                        for b in range(2):
                            w = conv_w[:, 2 * j + b, tap:tap + 1]
                            if tap == 0:
                                i = dve.tensor_scalar(yconv[:, b, :], raw[:, b, 0:TOK], w, None, ALU.mult)
                            else:
                                i = dve.scalar_tensor_tensor(out=yconv[:, b, :], in0=raw[:, b, tap:tap + TOK], scalar=w,
                                                             in1=yconv[:, b, :], op0=ALU.mult, op1=ALU.add)
                            if b == 1 and tap < 3:
                                link(i)
                    i.then_inc(conv_ok, 1)
                    prep(p + 2, par)
                    if j < TT:
                        post_tile(1 + h, j)
                for j in range(2):
                    p = p0 + 6 + j
                    dve.wait_ge(act_evac, p + 1 - MID_SKIP)
                    dve.tensor_scalar(zT[:, 2 * j:2 * j + 2, :], zT[:, 2 * j:2 * j + 2, :], ngain[:], None, ALU.mult).then_inc(acc_free, 1)
                    prep(p + 2, p % 2)
                p = p0 + GDN_STEPS
                dve.wait_ge(act_evac, p + 1 - MID_SKIP)
                dve.tensor_copy(arena[0:8, 15, :], arena[0:8, 14, :]).then_inc(acc_free, 1)

            def hv(i):
                return arena[:, i, :].rearrange("p (h c) -> p h c", h=GH)

            def sv(b):
                return side[:, b, :].rearrange("p (h c) -> p h c", h=GH)

            def gdn(h):
                c4 = lambda v: v.rearrange("p (l h) -> p l h", h=GH)
                dtb = dt_row[:].unsqueeze(1).to_broadcast([P, TT, GH])
                nab = neg_a[:].unsqueeze(1).to_broadcast([P, TT, GH])
                ab = sm[:, 16:18, :].rearrange("p a n -> p (a n)").rearrange("p (l e) -> p l e", e=8)
                g, be, eb, u = sm[:, 0, :], sm[:, 1, :], sm[:, 2, :], sm[:, 3, :]
                xx, q, z, z2 = sm[:, 7, :], sm[:, 8, :], sm[:, 9, :], sm[:, 11, :]
                dve.wait_ge(delta["ab_sbuf"], h + 1)
                link(dve.tensor_tensor(c4(xx), ab[:, :, 0:GH], dtb, ALU.add))
                link(dve.tensor_scalar(c4(eb), ab[:, :, GH:2 * GH], -1.0, 80.0, ALU.mult, ALU.min))
                dve.scalar_tensor_tensor(out=u, in0=xx, scalar=-1.0, in1=xx, op0=ALU.mult, op1=ALU.min).then_inc(delta["ab_exp"], 1)
                dve.wait_ge(delta["ab_exp"], 2 * h + 2)
                link(dve.tensor_scalar(eb, eb, 1.0, None, ALU.add))
                link(dve.reciprocal(be, eb))
                link(dve.tensor_scalar(q, u, 2.0, None, ALU.add))
                link(dve.reciprocal(z2, q))
                link(dve.tensor_tensor(z, u, z2, ALU.mult))
                link(dve.tensor_tensor(z2, z, z, ALU.mult))
                link(dve.tensor_scalar(q, z2, 1.0 / 15, None, ALU.mult))
                for odd in (13, 11, 9, 7, 5, 3):
                    link(dve.scalar_tensor_tensor(out=q, in0=q, scalar=1.0 / odd, in1=z2, op0=ALU.add, op1=ALU.mult))
                link(dve.scalar_tensor_tensor(out=q, in0=q, scalar=1.0, in1=z, op0=ALU.add, op1=ALU.mult))
                link(dve.tensor_scalar(xx, xx, 0.0, None, ALU.max))
                link(dve.scalar_tensor_tensor(out=q, in0=q, scalar=2.0, in1=xx, op0=ALU.mult, op1=ALU.add))
                dve.wait_ge(neg_rdy, 1)
                link(dve.tensor_tensor(c4(q), c4(q), nab, ALU.mult))
                dve.tensor_scalar(g, q, -1.0, None, ALU.mult).then_inc(delta["g_ready"], 1)
                dve.wait_ge(delta["g_sums"], h + 1)
                link(dve.tensor_copy(sm[:, 7, :], side[:, 1, 0:16]))
                link(dve.tensor_copy(sm[:, 8, :], side[:, 2, 0:16]))
                dve.tensor_tensor(sm[:, 9, :], sm[:, 8, :], sm[:, 7, :], ALU.subtract).then_inc(delta["g_exp"], 1)
                dve.wait_ge(delta["g_exp"], 2 * h + 2)
                dve.tensor_tensor(sm[:, 15, :], sm[:, 4, :], be, ALU.mult).then_inc(delta["beta_decay"], 1)
                def fv(b):
                    return front_bank(b)[:].rearrange("p (h c) -> p h c", h=GH)

                def front(l, stage):
                    n = h * TT + l
                    cs = slice(l * 4, l * 4 + 4)
                    if stage == 0:
                        dve.tensor_copy(hv(QN), bc_h(g[:, cs])).then_inc(delta["g_spread"], 1)
                    elif stage == 1:
                        dve.wait_ge(delta["squares"], 2 * n + 1)
                        dve.tensor_reduce(sm[:, 10, 0:4], hv(DECAY), AXX, ALU.add).then_inc(delta["sumsq"], 1)
                        dve.wait_ge(delta["squares"], 2 * n + 2)
                        dve.tensor_reduce(sm[:, 10, 4:8], hv(a_of(n)), AXX, ALU.add).then_inc(delta["sumsq"], 1)
                    elif stage == 2:
                        ex = arena[:, qk_of(n), :]
                        dve.wait_ge(delta["tok_major"], 4 * n + 4)
                        link(dve.tensor_tensor(hv(qk_of(n)), fv(3), bc_h(sm[:, 7, cs]), ALU.subtract))
                        dve.scalar_tensor_tensor(out=ex, in0=ex, scalar=-1.0, in1=ex,
                                                 op0=ALU.mult, op1=ALU.min).then_inc(delta["decay_exp"], 1)
                        dve.tensor_tensor(chunk_of(l, 2), fv(2), bc_h(be[:, cs]), ALU.mult).then_inc(delta["beta_v"], 1)
                    elif stage == 3:
                        dve.wait_ge(delta["roots"], n + 1)
                        dve.tensor_tensor(hv(QN), fv(0), bc_h(sm[:, 13, 0:4]), ALU.mult).then_inc(delta["qk_normed"], 1)
                        dve.tensor_tensor(hv(KN), fv(1), bc_h(sm[:, 13, 4:8]), ALU.mult).then_inc(delta["qk_normed"], 1)
                    elif stage == 5:
                        dve.wait_ge(delta["kk_qk"], n + 1)
                        dve.wait_ge(delta["decay_masked"], 4 * n + 3)
                        dve.tensor_tensor(hv(a_of(n)), fv(2), hv(a_of(n)), ALU.mult).then_inc(delta["A_ready"], 1)
                        dve.tensor_tensor(hv(qk_of(n)), fv(3), hv(qk_of(n)), ALU.mult).then_inc(delta["qk_masked"], 1)

                def output(l, part):
                    n = h * TT + l
                    if part == 0:
                        dve.wait_ge(delta["out_squares"], n + 1)
                        dve.tensor_reduce(sm[:, 14, 4:8], chunk_of(l, 1), AXX, ALU.add).then_inc(delta["out_sumsq"], 1)
                    elif part == 1:
                        dve.wait_ge(delta["out_roots"], n + 1)
                        dve.tensor_tensor(chunk_of(l, 2), chunk_of(l, 0), bc_h(sm[:, 14, 8:12]), ALU.mult).then_inc(delta["out_normed"], 1)
                    else:
                        dve.wait_ge(delta["outT_psum"], n + 1)
                        dve.tensor_tensor(zT[:, :, l * P:(l + 1) * P], sv(3), zT[:, :, l * P:(l + 1) * P], ALU.mult).then_inc(delta["gated"], 1)

                for stage in range(len(LEVELS)):
                    front(0, stage)
                for l in range(TT):
                    n = h * TT + l
                    cs = slice(l * 4, l * 4 + 4)
                    dve.wait_ge(delta["A_ready"], n + 1)
                    link(dve.tensor_tensor(hv(T_), hv(a_of(n)), bc_m(m_lvl[:, 0, :]), ALU.mult))
                    dve.tensor_tensor(hv(T_), bc_m(ident[:]), hv(T_), ALU.subtract).then_inc(delta["T_first"], 1)
                    if l + 1 < TT:
                        front(l + 1, 0)
                    for v, s in enumerate(LEVELS):
                        m = 6 * n + v
                        dve.wait_ge(delta["UAU_psum"], m + 1)
                        u_s = pairs_of(arena[:, U_, :], s, 1)
                        dve.tensor_tensor(u_s, u_s, pairs_of(side[:, 1, :], s, 1), ALU.subtract).then_inc(delta["U_level"], 1)
                        if v < len(LEVELS) - 1:
                            dve.wait_ge(delta["T_psum"], 5 * n + v + 1)
                            dve.tensor_copy(pairs_of(arena[:, T_, :], s, 0), pairs_of(side[:, 2, :], s, 0)).then_inc(delta["T_level"], 1)
                        if l and v in (0, 1, 3):
                            output(l - 1, (0, 1, 3).index(v))
                        if v and l + 1 < TT:
                            front(l + 1, v)
                    dve.wait_ge(delta["kS_qS"], n + 1)
                    link(dve.tensor_tensor(hv(R_), sv(0), bc_h(sm[:, 15, cs]), ALU.mult))
                    dve.tensor_tensor(hv(R_), chunk_of(l, 2), hv(R_), ALU.subtract).then_inc(delta["R_ready"], 1)
                    link(dve.tensor_tensor(chunk_of(l, 0), sv(3), bc_h(sm[:, 4, cs]), ALU.mult))
                    dve.wait_ge(delta["out_psum"], n + 1)
                    dve.wait_ge(delta["state_decayed"], n + 1)
                    dve.tensor_tensor(state[:], state[:], sv(0), ALU.add).then_inc(delta["state_ready"], 1)
                    dve.tensor_tensor(chunk_of(l, 0), chunk_of(l, 0), sv(2), ALU.add).then_inc(delta["out_sbuf"], 1)
                for part in range(3):
                    output(TT - 1, part)

            def log_counts(h, part):
                dd = arena[:, 0:2, :].rearrange("p a n -> p (a n)")
                m4 = arena[:, 2:4, :].rearrange("p a n -> p (a n)")
                m16 = arena[:, 4:6, :].rearrange("p a n -> p (a n)")
                lm = arena[:, 12:14, :].rearrange("p a n -> p (a n)")
                di = dd.bitcast(I32)
                ti = lm.bitcast(I32)
                if part == 1:
                    link(dve.scalar_tensor_tensor(out=m4, in0=di, scalar=0.0, in1=m4, op0=ALU.is_ge, op1=ALU.mult))
                    link(dve.tensor_scalar(lm, m4, 2.0, 8 * math.log(2.0), ALU.is_ge, ALU.mult))
                    link(dve.tensor_scalar(m16, m4, 3.0, 8 * math.log(1.5), ALU.is_ge, ALU.mult))
                    link(dve.tensor_tensor(lm, lm, m16, ALU.add))
                    link(dve.tensor_scalar(m4, m4, 1.0, NEG, ALU.is_lt, ALU.mult))
                    dve.tensor_tensor(lm, lm, m4, ALU.add).then_inc(attn["log_count"], 1)
                    return
                dve.wait_ge(attn["distance"], h + 1)
                link(dve.tensor_scalar(ti, di, 3, None, ALU.bitwise_and))
                link(dve.tensor_scalar(m4, ti, 0.0, None, ALU.is_equal))
                link(dve.tensor_scalar(ti, di, 15, None, ALU.bitwise_and))
                link(dve.tensor_scalar(m16, ti, 0.0, None, ALU.is_equal))
                link(dve.scalar_tensor_tensor(out=m4, in0=di, scalar=512.0, in1=m4, op0=ALU.is_le, op1=ALU.mult))
                link(dve.tensor_tensor(m4, m4, m16, ALU.add))
                link(dve.scalar_tensor_tensor(out=m4, in0=di, scalar=128.0, in1=m4, op0=ALU.is_le, op1=ALU.add))

            def att(h):
                n_units = AH * TT
                dve.wait_ge(delta["out_squares"], (h + 1) * TT)
                dve.wait_ge(delta["mix_hi"], h + 1)
                lo_of(h_lo[:, 0:4, :], zT[:], h_hi[:, 0:4, :], delta["mix_lo"])

                def smax(u):
                    n = h * n_units + u
                    hd, i = u // TT, u % TT
                    nk = h * TT + i + 1
                    sc, ptb, ob = bank(n)
                    sbuf = arena[:, 4 + 2 * (n % 2):6 + 2 * (n % 2), :].rearrange("p a n -> p (a n)")
                    bias = arena[:, 2 * (hd % 2):2 * (hd % 2) + 2, :].rearrange("p a n -> p (a n)")
                    b0 = S - nk * P
                    dve.wait_ge(attn["bias"], 3 * (h * AH + hd) + 3)
                    dve.wait_ge(attn["scores"], n + 1)
                    if u >= 2:
                        dve.wait_ge(attn["pT_psum"], PT_N[h] + (h + 1) * (u - 1))
                    for hh in range(h + 1):
                        m = min(nk - hh * TT, TT) * P
                        i_ = dve.tensor_tensor_reduce(sbuf[:, hh * TOK:hh * TOK + m], sc[hh][:, 0:m],
                                                      bias[:, b0 + hh * TOK:b0 + hh * TOK + m], 1.0, NEG, ALU.add, ALU.max,
                                                      sm[:, 18, 2 * (n % 2) + hh:2 * (n % 2) + hh + 1])
                    i_.then_inc(attn["max"], 1)
                    dve.wait_ge(attn["max"], n + 1)
                    mx = sm[:, 18, 2 * (n % 2):2 * (n % 2) + 1]
                    if h:
                        link(dve.tensor_tensor(mx, mx, sm[:, 18, 2 * (n % 2) + 1:2 * (n % 2) + 2], ALU.max))
                    dve.tensor_scalar(sm[:, 19, n % 2:n % 2 + 1], mx, -(AD ** -0.5), None, ALU.mult).then_inc(attn["neg_max"], 1)

                def fin(u):
                    n = h * n_units + u
                    hd, i = u // TT, u % TT
                    dve.wait_ge(attn["probs"], n + 1)
                    link(dve.reciprocal(sm[:, 22, n % 4:n % 4 + 1], sm[:, 20, n % 4:n % 4 + 1]))
                    dve.wait_ge(attn["out_psum"], n + 1)
                    dve.tensor_scalar(onat[:, i, hd * AD:(hd + 1) * AD], bank(n)[2][:, 0:AD], sm[:, 22, n % 4:n % 4 + 1],
                                      None, ALU.mult).then_inc(attn["out_sbuf"], 1)

                smax(0)
                smax(1)
                for u in range(n_units):
                    if u + 2 < n_units:
                        smax(u + 2)
                    fin(u)
                for b in range(4):
                    dve.wait_ge(attn["out_hi"], h * 4 + b + 1)
                    lo_of(h_lo[:, 4 + b, :], side[:, b % 2, :], h_hi[:, 4 + b, :], attn["out_lo"])

            def mem(h):
                n_units = MH * TT
                def mx(u):
                    n = h * n_units + u
                    dve.wait_ge(memo["scores"], n + 1)
                    link(dve.tensor_reduce(sm[:, 18, n % 2:n % 2 + 1], side[:, u % 2, 0:NMEM], AXX, ALU.max))
                    dve.tensor_scalar(sm[:, 19, n % 2:n % 2 + 1], sm[:, 18, n % 2:n % 2 + 1], -(MD ** -0.5), None, ALU.mult).then_inc(memo["neg_max"], 1)

                def normed(u):
                    n = h * n_units + u
                    dve.wait_ge(memo["probs"], n + 1)
                    link(dve.reciprocal(sm[:, 22, n % 2:n % 2 + 1], sm[:, 20, n % 2:n % 2 + 1]))
                    dve.tensor_scalar(arena[:, u % 2, 0:NMEM], arena[:, u % 2, 0:NMEM], sm[:, 22, n % 2:n % 2 + 1], None, ALU.mult).then_inc(memo["probs_normed"], 1)

                mx(0)
                mx(1)
                normed(0)
                for u in range(n_units):
                    hd, i = u // TT, u % TT
                    if u + 1 < n_units:
                        normed(u + 1)
                    if u + 2 < n_units:
                        mx(u + 2)
                    if i == TT - 1:
                        for d in range(2):
                            o = h * 8 + 2 * hd + d
                            dve.wait_ge(memo["out_hi"], o + 1)
                            lo_of(h_lo[:, 2 * hd + d, :], accp[d][0][:], h_hi[:, 2 * hd + d, :], memo["out_lo"])

            pre_a(0)
            prep(0, 0)
            dve.wait_ge(const_in, 16 * N_SMALL)
            pre_b(0)
            u0 = ffn(FFN1_0, FFN1_SKIP, 0, 0, None, 1)
            u0 = ffn(FFN1_0 + FFN_STEPS, FFN1_SKIP, 1, u0, 0, 2)
            dve.wait_ge(mask_st, N_CONST)
            for h in range(HALVES):
                p = MIX_0 + h * MIX_STEPS + GDN_STEPS + 1
                mix_in(h)
                gdn(h)
                plain(p, 2, qbT)
                log_counts(h, 0)
                plain(p + 2, 2, kb[h])
                log_counts(h, 1)
                plain(p + 4, 2, arena[:, 8:12, :])
                att(h)
                plain(p + ATT_STEPS, KT // 2, oT, q_next=3 + h)
                pre_b(3 + h)
            plain(KV_0, KT // 2, kmT, NMEM, r_prev=3, two=True)
            plain(KV_0 + KT // 2, KT // 2, qmT, NMEM, q_next=5, ahead=True, two=True)
            pre_b(5)
            for h in range(HALVES):
                p0 = MEM_0 + h * MEM_STEPS
                plain(p0, KT // 2, qmT, r_prev=4 if h else None, ahead=(h == 0), two=(h == 1))
                mem(h)
                plain(p0 + KT // 2, KT // 2, oT, q_next=6 + h, ahead=(h == 1))
                pre_b(6 + h)
            u0 = ffn(FFN2_0, FFN2_SKIP, 0, u0, 5, 8)
            u0 = ffn(FFN2_0 + FFN_STEPS, FFN2_SKIP, 1, u0, 6, None)
            for k in range(TT):
                post_tile(7, k)


_INS = ["x", "mem", "ffn1_pre_g", "ffn1_w_gate", "ffn1_w_up", "ffn1_w_down", "ffn1_post_g",
        "mix_pre_g", "w_in", "gdn_conv_w", "gdn_a_log", "gdn_dt_bias", "gdn_norm_g", "w_out", "mix_post_g",
        "mem_pre_g", "mem_kv_g", "mem_wq", "mem_wk", "mem_wv", "mem_wo", "mem_post_g",
        "ffn2_pre_g", "ffn2_w_gate", "ffn2_w_up", "ffn2_w_down", "ffn2_post_g"]


def kernel(**inputs):
    import numpy as np
    import concourse.bacc as bacc
    from concourse.bass_utils import run_bass_kernel_spmd

    nc = bacc.Bacc("TRN2", target_bir_lowering=False, num_devices=1)
    arrays, aps = {}, {}
    for name in _INS:
        a = np.ascontiguousarray(inputs[name])
        arrays["in_" + name] = a
        aps[name] = nc.dram_tensor("in_" + name, a.shape, mybir.dt.from_np(a.dtype), kind="ExternalInput").ap()
    aps["out"] = nc.dram_tensor("out_x", (1, S, D), F32, kind="ExternalOutput").ap()
    with nc.allow_non_contiguous_dma(reason="small gains, channels onto partitions"):
        hybrid_layer(nc, aps)
    got = run_bass_kernel_spmd(nc, [arrays], core_ids=[0])
    return got.results[0]["out_x"]
```
